# Optimizing a Trainium2 kernel written in Bass

```python
import jax, jax.numpy as jnp
from jax import lax
import numpy as np

D_MODEL = 1024
BATCH = 1
SEQ = 512
DEPTH = 1

CHUNK = 64
WINDOW = 128
WIN_CHUNKS = WINDOW // CHUNK
BAND = WIN_CHUNKS * CHUNK
MEM_LEN = 256

HD = 64
N_HEADS = 8
N_KV = 2
GQA = N_HEADS // N_KV
ATT_W = N_HEADS * HD
KV_W = N_KV * HD

CONV_W = 512
CONV_K = 3

MEM_HEADS = 4
MEM_HD = 128
MEM_W = MEM_HEADS * MEM_HD

N_BRANCH = 3
GATE_W = N_BRANCH * D_MODEL
IN_SPLITS = [CONV_W, CONV_W, CONV_W, ATT_W, KV_W, KV_W, MEM_W, GATE_W]
IN_W = sum(IN_SPLITS)

D_FF = 2816
FFN_K = 3

REL_BUCKETS = 32
REL_MAX_DIST = 128
EPS = 1e-6
NEG_INF = -1e30

kernel_name = "hybrid_conv_swa_memory_gated_trunk"

def rms_norm(x, g):
    x32 = x.astype(jnp.float32)
    y = x32 * lax.rsqrt(jnp.mean(x32 * x32, axis=-1, keepdims=True) + EPS)
    return (y * g.astype(jnp.float32)).astype(x.dtype)

def causal_dwconv(x, w, b=None):
    k, c = w.shape
    y = lax.conv_general_dilated(
        x, w[:, None, :].astype(x.dtype), window_strides=(1,), padding=[(k - 1, 0)],
        dimension_numbers=("NWC", "WIO", "NWC"), feature_group_count=c)
    if b is not None:
        y = y + b.astype(x.dtype)
    return y

def t5_buckets(rel):
    nb = REL_BUCKETS // 2
    bucket = (rel > 0).astype(np.int32) * nb
    n = np.abs(rel)
    max_exact = nb // 2
    large = max_exact + (np.log(np.maximum(n, 1) / max_exact) / np.log(REL_MAX_DIST / max_exact)
                         * (nb - max_exact)).astype(np.int32)
    large = np.minimum(large, nb - 1)
    return (bucket + np.where(n < max_exact, n, large)).astype(np.int32)

def shift_chunks(t, w):
    if w == 0:
        return t
    return jnp.concatenate([jnp.zeros_like(t[:, :w]), t[:, :-w]], axis=1)

def sliding_window_attention(q, k, v, rel_bias, sinks):
    bsz, s = q.shape[0], q.shape[1]
    nc = s // CHUNK
    q = q.reshape(bsz, nc, CHUNK, N_KV, GQA, HD)
    k = k.reshape(bsz, nc, CHUNK, N_KV, HD)
    v = v.reshape(bsz, nc, CHUNK, N_KV, HD)
    shifts = list(range(WIN_CHUNKS - 1, -1, -1))
    kb = jnp.concatenate([shift_chunks(k, w) for w in shifts], axis=2)
    vb = jnp.concatenate([shift_chunks(v, w) for w in shifts], axis=2)
    scores = jnp.einsum("bnqhgd,bnkhd->bnhgqk", q, kb).astype(jnp.float32) * (HD ** -0.5)
    qi = np.arange(CHUNK)[:, None]
    kj = np.arange(BAND)[None, :]
    rel = (kj - (WIN_CHUNKS - 1) * CHUNK) - qi
    bias = rel_bias.astype(jnp.float32)[t5_buckets(rel)]
    bias = jnp.transpose(bias, (2, 0, 1)).reshape(N_KV, GQA, CHUNK, BAND)
    slot_shift = (WIN_CHUNKS - 1) - np.arange(BAND) // CHUNK
    valid = (np.arange(nc)[:, None] - slot_shift[None, :]) >= 0
    scores = jnp.where(valid[None, :, None, None, None, :], scores + bias, NEG_INF)
    sink = sinks.astype(jnp.float32).reshape(N_KV, GQA)[..., None, None]
    m = jnp.maximum(jnp.max(scores, axis=-1, keepdims=True), sink)
    p = jnp.exp(scores - m)
    probs = p / (jnp.sum(p, axis=-1, keepdims=True) + jnp.exp(sink - m))
    out = jnp.einsum("bnhgqk,bnkhd->bnqhgd", probs.astype(vb.dtype), vb)
    return out.reshape(bsz, s, ATT_W)

def memory_attention(q, mk, mv):
    s = jnp.einsum("bshd,bmhd->bhsm", q, mk).astype(jnp.float32) * (MEM_HD ** -0.5)
    p = jax.nn.softmax(s, axis=-1)
    out = jnp.einsum("bhsm,bmhd->bshd", p.astype(mv.dtype), mv)
    return out.reshape(q.shape[0], q.shape[1], MEM_W)

def setup_inputs(seed: int = 0) -> dict:
    key = jax.random.key(seed)
    ks = jax.random.split(key, 24)

    def nrm(k, shape, scale):
        return jax.random.normal(k, shape, jnp.float32) * scale

    def gain(k, shape):
        return 1.0 + 0.02 * jax.random.normal(k, shape, jnp.float32)

    L = DEPTH
    return {
        "x": nrm(ks[0], (BATCH, SEQ, D_MODEL), 1.0),
        "mem": nrm(ks[1], (BATCH, MEM_LEN, D_MODEL), 1.0),
        "rel_bias": nrm(ks[2], (REL_BUCKETS, N_HEADS), 0.5),
        "norm_mix": gain(ks[3], (L, D_MODEL)),
        "norm_mem": gain(ks[4], (L, D_MODEL)),
        "norm_ffn": gain(ks[5], (L, D_MODEL)),
        "w_in": nrm(ks[6], (L, D_MODEL, IN_W), D_MODEL ** -0.5),
        "b_gate": nrm(ks[7], (L, GATE_W), 0.1),
        "conv_w": nrm(ks[8], (L, CONV_K, CONV_W), CONV_K ** -0.5),
        "q_norm": gain(ks[9], (L, HD)),
        "k_norm": gain(ks[10], (L, HD)),
        "sinks": nrm(ks[11], (L, N_HEADS), 0.5),
        "mq_norm": gain(ks[12], (L, MEM_HD)),
        "mk_norm": gain(ks[13], (L, MEM_HD)),
        "w_mem_kv": nrm(ks[14], (L, D_MODEL, 2 * MEM_W), D_MODEL ** -0.5),
        "w_br_conv": nrm(ks[15], (L, CONV_W, D_MODEL), CONV_W ** -0.5),
        "w_br_attn": nrm(ks[16], (L, ATT_W, D_MODEL), ATT_W ** -0.5),
        "w_br_mem": nrm(ks[17], (L, MEM_W, D_MODEL), MEM_W ** -0.5),
        "w_o": nrm(ks[18], (L, D_MODEL, D_MODEL), D_MODEL ** -0.5),
        "w_up": nrm(ks[19], (L, D_MODEL, 2 * D_FF), D_MODEL ** -0.5),
        "ffn_conv_w": nrm(ks[20], (L, FFN_K, 2 * D_FF), FFN_K ** -0.5),
        "ffn_conv_b": nrm(ks[21], (L, 2 * D_FF), 0.02),
        "w_down": nrm(ks[22], (L, D_FF, D_MODEL), D_FF ** -0.5),
    }

def reference(x, mem, rel_bias, norm_mix, norm_mem, norm_ffn, w_in, b_gate, conv_w,
              q_norm, k_norm, sinks, mq_norm, mk_norm, w_mem_kv, w_br_conv, w_br_attn,
              w_br_mem, w_o, w_up, ffn_conv_w, ffn_conv_b, w_down):
    bsz, s = x.shape[0], x.shape[1]
    cuts = list(np.cumsum(IN_SPLITS)[:-1])
    for l in range(DEPTH):
        h = rms_norm(x, norm_mix[l])
        proj = jnp.einsum("bsd,de->bse", h, w_in[l])
        b_c, c_c, x_c, q, k, v, mq, g = jnp.split(proj, cuts, axis=-1)

        u = causal_dwconv(c_c * x_c, conv_w[l])
        y_conv = jnp.einsum("bsc,cd->bsd", b_c * u, w_br_conv[l])

        q = rms_norm(q.reshape(bsz, s, N_HEADS, HD), q_norm[l])
        k = rms_norm(k.reshape(bsz, s, N_KV, HD), k_norm[l])
        v = v.reshape(bsz, s, N_KV, HD)
        a = sliding_window_attention(q, k, v, rel_bias, sinks[l])
        y_attn = jnp.einsum("bsc,cd->bsd", a, w_br_attn[l])

        mh = rms_norm(mem, norm_mem[l])
        mkv = jnp.einsum("bmd,de->bme", mh, w_mem_kv[l])
        mk, mv = jnp.split(mkv, 2, axis=-1)
        mk = rms_norm(mk.reshape(bsz, MEM_LEN, MEM_HEADS, MEM_HD), mk_norm[l])
        mv = mv.reshape(bsz, MEM_LEN, MEM_HEADS, MEM_HD)
        mq = rms_norm(mq.reshape(bsz, s, MEM_HEADS, MEM_HD), mq_norm[l])
        y_mem = jnp.einsum("bsc,cd->bsd", memory_attention(mq, mk, mv), w_br_mem[l])

        g_conv, g_attn, g_mem = jnp.split(jax.nn.sigmoid(g + b_gate[l]), N_BRANCH, axis=-1)
        merged = g_conv * y_conv + g_attn * y_attn + g_mem * y_mem
        x = x + jnp.einsum("bsd,de->bse", merged, w_o[l])

        h = rms_norm(x, norm_ffn[l])
        up = causal_dwconv(jnp.einsum("bsd,df->bsf", h, w_up[l]), ffn_conv_w[l], ffn_conv_b[l])
        gt, val = jnp.split(up, 2, axis=-1)
        x = x + jnp.einsum("bsf,fd->bsd", jax.nn.silu(gt) * val, w_down[l])
    return x


_drawn_inputs = setup_inputs


def setup_inputs(seed=0):
    import zlib

    import numpy as np

    out = dict(_drawn_inputs(seed))
    spreads = {}
    factors = {'norm_mix': 3.233,
     'norm_mem': 8.0,
     'norm_ffn': 16.496,
     'b_gate': 2.757,
     'q_norm': 31.292,
     'k_norm': 30.592,
     'sinks': 8.0,
     'mq_norm': 8.0,
     'mk_norm': 8.0,
     'ffn_conv_b': 16.676,
     'rel_bias': 36.858}
    for name, (base, spread) in spreads.items():
        noise = np.random.default_rng([zlib.crc32(name.encode()), seed]).standard_normal(out[name].shape)
        drawn = base * np.exp(spread * noise) if base else spread * noise
        out[name] = __import__('jax').numpy.asarray(drawn.astype(out[name].dtype))
    for name, factor in factors.items():
        out[name] = (out[name] * factor).astype(out[name].dtype)
    return out
```

```python
import concourse.bass as bass
from concourse import mybir
from contextlib import ExitStack

P = 128
SEQ, D, MEM = 512, 1024, 256
KD = D // P
TT = SEQ // P
MT = MEM // P
HD, NH, NKV, MH, MHD = 64, 8, 2, 4, 128
GQA = NH // NKV
CONV_W, FF = 512, 2816
CB = CONV_W // P
FB = FF // P
CHUNK = 64
WIN = 3 * CHUNK
ATT0 = 3 * CONV_W
KV0 = ATT0 + NH * HD
MQ0 = KV0 + 2 * NKV * HD
GATE0 = MQ0 + MH * MHD
EPS = 1e-6
MASKED = -1e30
REL = P + WIN

N_MEMK, N_MEMV, N_Q, N_KVM, N_MQ2, N_CONV = 0, 4, 8, 12, 16, 18
N_J, J_WT, J_IT = 30, 9, KD // 2
N_WO = N_J + J_WT * J_IT
N_UP, UP_IT = N_WO + 8, FB // 2
N_DN, DN_IT = N_UP + 4 * UP_IT, (FB // 2 - 3) // 2
N_END = N_DN + FB


def slot_of(n):
    return n % 3 if n < N_WO else (n - N_WO) % 4


def uses(n):
    return sum(slot_of(m) == slot_of(n) for m in range(n + 1))


def previous(n):
    before = [m for m in range(n) if slot_of(m) == slot_of(n)]
    return before[-1] if before else None


ATTEND, MEM_SCORES, MEM_ATTEND = (20, 23, 26, 29), (19, 22, 25, 27), (21, 24, 27, 29)


def straight_results():
    out, turn = [], [0]

    def side(*name):
        out.append((name, 4 + turn[0] % 4))
        turn[0] += 1

    def scores(t):
        for g in range(NKV):
            for r in range(2):
                side("score", t, g, r)

    def probs(t):
        for kt in ((0, 1) if t else (1,)):
            for g in range(NKV):
                side("probT", t, kt, g)
        side("attn", t)

    def mem_scores(t):
        side("mscore", t, 0)
        side("mscore", t, 1)

    def mem_probs(t):
        side("mprobT", t, 0)
        side("mprobT", t, 1)
        side("mattn", t)

    for t in range(MT):
        side("memT", t, 0)
        side("memT", t, 1)
    for n in range(N_MEMK, N_MEMV):
        if n == N_MEMV - 1:
            out.append((("mk", 0), 0))
            out.append((("mk", 1), 1))
        else:
            out.append((("wt", n), None))
        if n == 0:
            side("params")
            side("relvec")
        if n >= 2:
            side("xT", n - 2, 0)
            side("xT", n - 2, 1)
    for n in range(N_MEMV, N_Q):
        if n == N_Q - 1:
            out.append((("mv", 0), 2))
            out.append((("mv", 1), 3))
        else:
            out.append((("wt", n), None))
        if n < 6:
            side("xT", n - 2, 0)
            side("xT", n - 2, 1)
        if n == 6:
            side("mkT", 0)
            side("mkT", 1)
    for first, last, name in ((N_Q, N_KVM, "q"), (N_KVM, N_MQ2, "kvm"), (N_MQ2, N_CONV, "mq2")):
        for n in range(first, last):
            if n == last - 1:
                for t in range(TT):
                    out.append(((name, t), t))
            else:
                out.append((("wt", n), None))
            if n == 10:
                for a in range(4):
                    side("bias", a)
            if n in (13, 14):
                side("qT", 2 * (n - 13))
                side("qT", 2 * (n - 13) + 1)
            if n in (16, 17):
                side("kmT", 2 * (n - 16))
                side("kmT", 2 * (n - 16) + 1)
            if n == 17:
                scores(0)
    for n in range(N_CONV, N_J):
        out.append((("conv", n), (n - N_CONV) % 4))
        if n == 18:
            side("mq2T", 0)
            side("mq2T", 1)
        if n in ATTEND:
            probs(ATTEND.index(n))
            if n != ATTEND[-1]:
                scores(ATTEND.index(n) + 1)
        if n in MEM_ATTEND:
            mem_probs(MEM_ATTEND.index(n))
        if n in MEM_SCORES:
            mem_scores(MEM_SCORES.index(n))
    return out


RESULTS = straight_results()
BANK = {name: bank for name, bank in RESULTS}
DONE = {name: i + 1 for i, (name, _) in enumerate(RESULTS)}
NTH = {name: sum(b == bank for _, b in RESULTS[:i + 1]) for i, (name, bank) in enumerate(RESULTS)}
TAKEN0 = [sum(b == bank for _, b in RESULTS) for bank in range(8)]
DONE0 = len(RESULTS)
J_DONE, UP_DONE, DN_DONE = 12, 4, 4
DONE_WO = DONE0 + J_DONE * J_IT
J_TAKEN = [2, 2, 2, 2, 1, 1, 1, 1]
TAKEN_WO = [a + J_IT * b for a, b in zip(TAKEN0, J_TAKEN)]
WO_ORDER = [("wo", 0), ("wo", 1), ("h2T", 0), ("wo", 2), ("h2T", 1), ("w", 70), ("w", 71), ("w", 72), ("wo", 3),
            ("h2T", 2), ("h2T", 3)]
WO_AT, _at = {}, DONE_WO + 7
for _name in WO_ORDER:
    _at += 2 if _name[0] == "h2T" else 1
    WO_AT[_name] = _at
DONE_UP = _at
TAKEN_UP = [TAKEN_WO[b] + (3 if b < 4 else 1) for b in range(8)]
DONE_DN = DONE_UP + UP_DONE * UP_IT
TAKEN_DN = [TAKEN_UP[b] + (UP_IT if b >= 4 else 0) for b in range(8)]


def last_name(n):
    if n == N_MEMV - 1:
        return ("mk", 1)
    if n == N_Q - 1:
        return ("mv", 1)
    for last, name in ((N_KVM, "q"), (N_MQ2, "kvm"), (N_CONV, "mq2")):
        if n == last - 1:
            return (name, TT - 1)
    return ("conv", n) if n >= N_CONV else ("wt", n)


NORMED_MK = MT + TT
NORMED_Q = NORMED_MK + MT
NORMED_KM, NORMED_MQ2, NORMED_H2 = NORMED_Q + TT, NORMED_Q + 2 * TT, NORMED_Q + 3 * TT
PARAM_DMAS = 11
J_USED = [1, 2, 3, 4, 5, 6, 8, 10, 12]


def used(n):
    if n < N_J:
        return DONE[last_name(n)]
    if n < N_WO:
        return DONE0 + (n - N_J) // J_WT * J_DONE + J_USED[(n - N_J) % J_WT]
    if n < N_WO + 3:
        return DONE_WO + n - N_WO + 1
    if n == N_WO + 3:
        return DONE_WO + 7
    if n < N_UP:
        return WO_AT[("w", n)] if n < N_UP - 1 else WO_AT[("wo", 3)]
    return DONE_UP + n - N_UP + 1


def line(value, n, i, period):
    step = value(n + 2 * period) - value(n + period)
    assert value(n + period) - step >= value(n)
    return value(n + period) - step + i * step


def trunk(nc, x, mem, rel_bias, norm_mix, norm_mem, norm_ffn, w_in, b_gate, conv_w, q_norm, k_norm, sinks,
          mq_norm, mk_norm, w_mem_kv, w_br_conv, w_br_attn, w_br_mem, w_o, w_up, ffn_conv_w, ffn_conv_b, w_down,
          eye, flip, bucket_of, out):
    f32, f32r = mybir.dt.float32, mybir.dt.float32r
    ALU, ACT, AX = mybir.AluOpType, mybir.ActivationFunctionType, mybir.AxisListType
    ds = bass.ds

    win_v = w_in[0].rearrange("(k p) c -> p k c", p=P)
    wkv_v = w_mem_kv[0].rearrange("(k p) c -> p k c", p=P)
    wbr_v = [w[0].rearrange("(k p) c -> p k c", p=P) for w in (w_br_conv, w_br_attn, w_br_mem)]
    wo_v = w_o[0].rearrange("(k p) c -> p k c", p=P)
    wup_v = w_up[0].rearrange("(k p) c -> p k c", p=P)
    wdn_v = w_down[0].rearrange("(k p) c -> p k c", p=P)
    x_v = x[0].rearrange("(t p) d -> p t d", p=P)
    mem_v = mem[0].rearrange("(t p) d -> p t d", p=P)
    out_v = out[0].rearrange("(t p) d -> p t d", p=P)
    rel_dram = nc.dram_tensor("rel_dram", (NH, REL), f32, kind="Internal").ap()

    ctx = ExitStack()
    with ctx:
        def sb(name, shape, dt):
            return ctx.enter_context(nc.sbuf_tensor(name, shape, dt))

        def sem(name):
            return ctx.enter_context(nc.semaphore(name))

        stage = sb("stage", [P, 4, 1024], f32)
        w_hi = sb("w_hi", [P, 4, 1024], f32r)
        w_lo = sb("w_lo", [P, 4, 1024], f32r)
        h_hi = sb("h_hi", [P, KD, SEQ], f32r)
        h_lo = sb("h_lo", [P, KD, SEQ], f32r)
        a_hi = sb("a_hi", [P, 12, SEQ], f32r)
        a_lo = sb("a_lo", [P, 12, SEQ], f32r)
        arena = sb("arena", [P, 16384], f32)
        temp = sb("temp", [P, 4, SEQ], f32)
        ident = sb("ident", [P, P], f32)
        cols = sb("cols", [P, 216], f32)
        stat = sb("stat", [P, 112], f32)

        x_t = arena[:, 0:4096].rearrange("p (t d) -> p t d", t=TT)
        qT = arena[:, 0:2048].rearrange("p (b s) -> p b s", b=4)
        mqT = arena[:, 2048:4096].rearrange("p (b s) -> p b s", b=4)
        raw_a = arena[:, 4096:6144].rearrange("p (t c) -> p t c", t=TT)
        probs = arena[:, 6144:8192].rearrange("p (h c) -> p h c", h=NH)
        raw_b = arena[:, 6144:8192].rearrange("p (t c) -> p t c", t=TT)
        mem_t = arena[:, 6144:8192].rearrange("p (t d) -> p t d", t=MT)
        rel_flip = arena[:, 6144:6144 + NH * WIN].rearrange("p (h c) -> p h c", h=NH)
        probT = arena[:, 4096:6144].rearrange("p (k g r c) -> p k g r c", k=2, g=NKV, r=2)
        kT = arena[:, 8192:9216].rearrange("p (g s) -> p g s", g=NKV)
        params = arena[:, 8192:8192 + 3 * P].rearrange("p (a c) -> p a c", a=3)
        mkT = arena[:, 9216:10240].rearrange("p (h s) -> p h s", h=MH)
        m_v = arena[:, 10240:11264].rearrange("p (t c) -> p t c", t=MT)
        v_t = arena[:, 11264:11776].rearrange("p (t c) -> p t c", t=TT)
        bias = arena[:, 11776:11776 + NH * WIN].rearrange("p (h c) -> p h c", h=NH)
        mprobs = arena[:, 13312:14336].rearrange("p (h c) -> p h c", h=MH)
        mprobT = arena[:, 14336:15360].rearrange("p (k c) -> p k c", k=2)
        gain_mem = arena[:, 13312:14336]
        gain_mix = arena[:, 14336:15360]
        mk_raw = arena[:, 15360:16384].rearrange("p (t c) -> p t c", t=MT)
        sig = arena[:, 0:3072].rearrange("p (b s) -> p b s", b=6)
        merged = arena[:, 4096:8192]
        merge_tmp = arena[:, 8192:9216].rearrange("p (b s) -> p b s", b=2)
        act = arena[:, 0:FB * SEQ]
        gain_ffn = arena[:, 11264:12288]
        x2 = arena[:, 12288:16384].rearrange("p (t d) -> p t d", t=TT)
        temp2 = temp[:, :, :].rearrange("p (a b) s -> p a (b s)", b=2)
        flip_sb = temp[:, 3, 0:P]
        onehot = temp[0:32, 2, 0:REL]
        rel_sb = temp[0:32, 3, P:P + NH]
        rel_row = temp[0:NH, 1, 0:REL]

        memT_hi = a_hi[:, 0:4, :].rearrange("p a b -> p (a b)").rearrange("p (k s) -> p k s", k=KD)
        memT_lo = a_lo[:, 0:4, :].rearrange("p a b -> p (a b)").rearrange("p (k s) -> p k s", k=KD)
        aring_hi = h_hi[:, 0:4, :].rearrange("p a b -> p (a b)")
        aring_lo = h_lo[:, 0:4, :].rearrange("p a b -> p (a b)")

        bg_col = cols[:, 0:24]
        cw_col = cols[:, 24:36]
        qg, kg, mqg, mkg = (cols[:, c:c + 1] for c in (36, 37, 38, 39))
        fb_col = cols[:, 40:40 + FB * 2]
        fw_col = cols[:, 84:84 + 3 * 2 * FB]
        neg_half = stat[:, 0:8]
        sink = stat[:, 8:16]
        ss = stat[:, 16:24]
        rstd = stat[:, 24:32]
        hv = stat[:, 32:64].rearrange("p (t c) -> p t c", t=TT)
        kv_ = stat[:, 64:80].rearrange("p (t c) -> p t c", t=TT)
        mk_ = stat[:, 64:72].rearrange("p (t c) -> p t c", t=MT)
        mq_ = stat[:, 80:88].rearrange("p (t c) -> p t c", t=TT)
        top, den = stat[:, 88:96], stat[:, 96:104]
        mtop, mden = stat[:, 104:108], stat[:, 108:112]
        sink_e = stat[:, 32:40]
        ss2a, ss2b, rstd2 = stat[:, 16:20], stat[:, 20:24], stat[:, 24:28]

        bank = [ctx.enter_context(nc.psum_tensor(f"bank{b}", [P, 512], f32)) for b in range(8)]

        w_loaded = [sem(f"w_loaded{s}") for s in range(4)]
        hi_ready = sem("hi_ready")
        lo_ready = sem("lo_ready")
        pe_done = sem("pe_done")
        taken = [sem(f"taken{b}") for b in range(8)]
        mem_in = [sem(f"mem_in{t}") for t in range(MT)]
        x_in = [sem(f"x_in{t}") for t in range(TT)]
        gains_in = sem("gains_in")
        eye_in = sem("eye_in")
        params_in = sem("params_in")
        rel_in = sem("rel_in")
        sink_in = sem("sink_in")
        relvec_out = sem("relvec_out")
        relflip_in = sem("relflip_in")
        x_again = sem("x_again")
        ffn_gain_in = sem("ffn_gain_in")
        stored = sem("stored")
        squares = sem("squares")
        var_ready = sem("var_ready")
        pow_ready = sem("pow_ready")
        normed = sem("normed")
        hi_taken = sem("hi_taken")
        sq_ready = sem("sq_ready")
        v_ready = sem("v_ready")
        params_done = sem("params_done")
        maxed = sem("maxed")
        expd = sem("expd")
        recip = sem("recip")
        probs_ready = sem("probs_ready")
        mmaxed = sem("mmaxed")
        mrecip = sem("mrecip")
        mprobs_ready = sem("mprobs_ready")
        zeroed = sem("zeroed")
        conv_hi = sem("conv_hi")
        conv_x = sem("conv_x")
        conv_lo = sem("conv_lo")
        merged_ready = sem("merged_ready")
        merged_hi = sem("merged_hi")
        merged_lo = sem("merged_lo")
        tap_ready = sem("tap_ready")
        silu_ready = sem("silu_ready")
        act_ready = sem("act_ready")
        ring_hi = sem("ring_hi")
        ring_lo = sem("ring_lo")
        final = sem("final")
        dve_chain = sem("dve_chain")

        block = ctx.enter_context(nc.Block())

        def matmul3(dst, stat_hi, stat_lo, mov_hi, mov_lo, first, last):
            nc.tensor.matmul(dst, stat_hi, mov_hi, start=first, stop=False)
            nc.tensor.matmul(dst, stat_hi, mov_lo, start=False, stop=False)
            return nc.tensor.matmul(dst, stat_lo, mov_hi, start=False, stop=last)

        def wait_taken(engine, name):
            engine.wait_ge(taken[BANK[name]], NTH[name])

        @block.tensor
        def _(pe):
            at = [0]

            def finished(name, ins):
                assert RESULTS[at[0]][0] == name, (RESULTS[at[0]], name)
                at[0] += 1
                ins.then_inc(pe_done, 1)

            def bank_for(name):
                b = BANK[name]
                if NTH[name] > 1:
                    pe.wait_ge(taken[b], NTH[name] - 1)
                return bank[b]

            def was_taken(name):
                wait_taken(pe, name)

            def transposes(name, sources, at_bank=None):
                ps = bank_for(name)
                for c, src in enumerate(sources):
                    last = nc.tensor.transpose(ps[:, c * P:(c + 1) * P], src, ident[:, :])
                finished(name, last)

            def tokens_stationary(n, first, last_n, names, lhs, width, count):
                kk = 1024 // width
                pe.wait_ge(lo_ready, n + 1)
                s = slot_of(n)
                for t in range(count):
                    if n == first:
                        bank_for(names[t])
                    for k in range(kk):
                        kb = (n - first) * kk + k
                        last = matmul3(bank[BANK[names[t]]][:, 0:width],
                                       lhs[0][:, kb, t * P:(t + 1) * P], lhs[1][:, kb, t * P:(t + 1) * P],
                                       w_hi[:, s, k * width:(k + 1) * width], w_lo[:, s, k * width:(k + 1) * width],
                                       kb == 0, kb == KD - 1)
                    if n == last_n:
                        finished(names[t], last)
                if n != last_n:
                    finished(("wt", n), last)

            def feature_block(ps, s, rhs, blocks=KD, width=P, c=0, start=0):
                for k in range(blocks):
                    a = k * width + c * P
                    last = matmul3(ps[:, :], w_hi[:, s, a:a + P], w_lo[:, s, a:a + P],
                                   rhs[0][:, start + k, :], rhs[1][:, start + k, :], k == 0, k == blocks - 1)
                return last

            pe.wait_ge(eye_in, 16)
            for t in range(MT):
                pe.wait_ge(normed, t + 1)
                for half in range(2):
                    transposes(("memT", t, half), [mem_t[:, t, (4 * half + c) * P:(4 * half + c + 1) * P]
                                                   for c in range(4)])
            for t in range(MT):
                for half in range(2):
                    was_taken(("memT", t, half))

            def x_transposes(t):
                pe.wait_ge(normed, MT + t + 1)
                for half in range(2):
                    transposes(("xT", t, half), [x_t[:, t, (4 * half + c) * P:(4 * half + c + 1) * P]
                                                 for c in range(4)])

            for n in range(N_MEMK, N_Q):
                first, name = (N_MEMK, "mk") if n < N_MEMV else (N_MEMV, "mv")
                tokens_stationary(n, first, first + 3, [(name, t) for t in range(MT)], (memT_hi, memT_lo), 512, MT)
                if n == 0:
                    pe.wait_ge(params_in, PARAM_DMAS * 16)
                    ps = bank_for(("params",))
                    nc.tensor.transpose(ps[:, 0:84], params[0:84, 0, :], ident[0:84, 0:84])
                    nc.tensor.transpose(ps[:, 84:172], params[0:88, 1, :], ident[0:88, 0:88])
                    finished(("params",), nc.tensor.transpose(ps[:, 172:216], params[0:44, 2, :], ident[0:44, 0:44]))
                    pe.wait_ge(rel_in, 48)
                    finished(("relvec",), nc.tensor.matmul(bank_for(("relvec",))[0:NH, 0:REL], rel_sb, onehot,
                                                           start=True, stop=True))
                if 2 <= n < 6:
                    x_transposes(n - 2)
                if n == 6:
                    for t in range(MT):
                        pe.wait_ge(normed, NORMED_MK + t + 1)
                        transposes(("mkT", t), [mk_raw[:, t, h * P:(h + 1) * P] for h in range(MH)])
            for t in range(TT):
                for half in range(2):
                    was_taken(("xT", t, half))
            h = (h_hi, h_lo)
            for n in range(N_Q, N_CONV):
                if n < N_KVM:
                    tokens_stationary(n, N_Q, N_KVM - 1, [("q", t) for t in range(TT)], h, 512, TT)
                elif n < N_MQ2:
                    tokens_stationary(n, N_KVM, N_MQ2 - 1, [("kvm", t) for t in range(TT)], h, 512, TT)
                else:
                    tokens_stationary(n, N_MQ2, N_CONV - 1, [("mq2", t) for t in range(TT)], h, 256, TT)
                if n == 10:
                    pe.wait_ge(relflip_in, 16)
                    for a in range(4):
                        name = ("bias", a)
                        ps = bank_for(name)
                        finished(name, nc.tensor.matmul(ps[:, 0:2 * WIN], flip_sb, rel_flip[:, 2 * a:2 * a + 2, :]
                                                        .rearrange("p h c -> p (h c)"), start=True, stop=True))
                if n in (13, 14):
                    for t in (2 * (n - 13), 2 * (n - 13) + 1):
                        pe.wait_ge(normed, NORMED_Q + t + 1)
                        transposes(("qT", t), [raw_a[:, t, c * P:(c + 1) * P] for c in range(4)])

                def key_transposes(t):
                    pe.wait_ge(normed, NORMED_KM + t + 1)
                    transposes(("kmT", t), [temp[:, t, 0:P], temp[:, t, P:2 * P],
                                            raw_b[:, t, 256:384], raw_b[:, t, 384:512]])
                if n in (16, 17):
                    key_transposes(2 * (n - 16))
                    key_transposes(2 * (n - 16) + 1)

            def scores(t):
                was_taken(("qT", t))
                was_taken(("kmT", t))
                lo = 0 if t else CHUNK
                for g in range(NKV):
                    for r in range(2):
                        name = ("score", t, g, r)
                        ps = bank_for(name)
                        for i in range(2):
                            last = nc.tensor.matmul(
                                ps[:, i * WIN + lo:(i + 1) * WIN],
                                qT[64 * r:64 * r + 64, 2 * g + i, t * P:(t + 1) * P],
                                kT[64 * r:64 * r + 64, g, t * P - CHUNK + lo:(t + 1) * P], start=True, stop=True)
                        finished(name, last)

            def attend(t):
                pe.wait_ge(probs_ready, t + 1)
                kts = (0, 1) if t else (1,)
                for kt in kts:
                    for g in range(NKV):
                        transposes(("probT", t, kt, g), [probs[:, 4 * g + 2 * i + r, kt * P:(kt + 1) * P]
                                                         for r in range(2) for i in range(2)])
                for kt in kts:
                    for g in range(NKV):
                        was_taken(("probT", t, kt, g))
                if t == 0:
                    pe.wait_ge(v_ready, TT)
                name = ("attn", t)
                ps = bank_for(name)
                for g in range(NKV):
                    for r in range(2):
                        for kt in kts:
                            last = nc.tensor.matmul(ps[64 * r:64 * r + 64, g * 256:(g + 1) * 256],
                                                    v_t[:, t - 1 + kt, g * HD:(g + 1) * HD],
                                                    probT[:, kt, g, r, :], start=(kt == kts[0]), stop=(kt == 1))
                finished(name, last)

            def mem_scores(t):
                for a in range(2):
                    name = ("mscore", t, a)
                    if a == 0:
                        was_taken(("mkT", 0))
                        was_taken(("mkT", 1))
                        was_taken(("kmT", t))
                    else:
                        was_taken(("mq2T", t // 2))
                    ps = bank_for(name)
                    for i in range(2):
                        last = nc.tensor.matmul(ps[:, i * MEM:(i + 1) * MEM], mqT[:, 2 * a + i, t * P:(t + 1) * P],
                                                mkT[:, 2 * a + i, :], start=True, stop=True)
                    finished(name, last)

            def mem_attend(t):
                pe.wait_ge(mprobs_ready, t + 1)
                for kt in range(2):
                    transposes(("mprobT", t, kt), [mprobs[:, i, kt * P:(kt + 1) * P] for i in range(MH)])
                for kt in range(2):
                    was_taken(("mprobT", t, kt))
                was_taken(("mv", 1))
                name = ("mattn", t)
                ps = bank_for(name)
                for i in range(MH):
                    for kt in range(2):
                        last = nc.tensor.matmul(ps[:, i * P:(i + 1) * P], m_v[:, kt, i * P:(i + 1) * P],
                                                mprobT[:, kt, i * P:(i + 1) * P], start=(kt == 0), stop=(kt == 1))
                finished(name, last)

            scores(0)
            for n in range(N_CONV, N_J):
                name = ("conv", n)
                ps = bank_for(name)
                pe.wait_ge(lo_ready, n + 1)
                finished(name, feature_block(ps, slot_of(n), h))
                if n == 18:
                    for a in range(2):
                        pe.wait_ge(normed, NORMED_MQ2 + 2 * a + 2)
                        transposes(("mq2T", a), [raw_a[:, 2 * a + tt, c * P:(c + 1) * P]
                                                 for tt in range(2) for c in range(2)])
                if n in ATTEND:
                    attend(ATTEND.index(n))
                    if n != ATTEND[-1]:
                        scores(ATTEND.index(n) + 1)
                if n in MEM_ATTEND:
                    mem_attend(MEM_ATTEND.index(n))
                if n in MEM_SCORES:
                    mem_scores(MEM_SCORES.index(n))
            assert at[0] == len(RESULTS)

            a_in = (a_hi, a_lo)
            def merge_pair(i):
                for r in range(J_WT):
                    n = N_J + r
                    pe.wait_ge(lo_ready, i * J_WT + n + 1)
                    if r < 6:
                        b = r % 4
                        pe.wait_ge(taken[b], i * J_TAKEN[b] + TAKEN0[b] + (r >= 4))
                        feature_block(bank[b], slot_of(n), h).then_inc(pe_done, 1)
                        continue
                    if r == 6:
                        pe.wait_ge(conv_lo, CB)
                    if r == 7:
                        for b in range(4, 8):
                            pe.wait_ge(taken[b], TAKEN0[b])
                    for jj in range(2):
                        b = 2 + 2 * (r - 6) + jj
                        pe.wait_ge(taken[b], i * J_TAKEN[b] + TAKEN0[b] + (b < 4))
                        feature_block(bank[b], slot_of(n), a_in, blocks=4, width=256, c=jj,
                                      start=4 * (r - 6)).then_inc(pe_done, 1)

            with pe.Fori(0, J_IT - 1) as i:
                merge_pair(i)
            merge_pair(J_IT - 1)

            def wo_part(n, t, b):
                kb = (n - N_WO) % 4 * 2
                for k in range(2):
                    last = matmul3(bank[b][:, :], h_hi[:, kb + k, t * P:(t + 1) * P], h_lo[:, kb + k, t * P:(t + 1) * P],
                                   w_hi[:, slot_of(n), k * 512:(k + 1) * 512], w_lo[:, slot_of(n), k * 512:(k + 1) * 512],
                                   kb + k == 0, kb + k == KD - 1)
                return last

            for n in range(N_WO, N_WO + 4):
                pe.wait_ge(lo_ready, n + 1)
                pe.wait_ge(merged_lo, 2 * (n - N_WO) + 2)
                for t in range(TT):
                    if n == N_WO:
                        pe.wait_ge(taken[t], TAKEN_WO[t])
                    last = wo_part(n, t, t)
                    if n == N_WO + 3:
                        last.then_inc(pe_done, 1)
                if n < N_WO + 3:
                    last.then_inc(pe_done, 1)
            for t in range(TT):
                pe.wait_ge(taken[4 + t], TAKEN_WO[4 + t])
                for n in range(N_WO + 4, N_UP):
                    if t == 0:
                        pe.wait_ge(lo_ready, n + 1)
                    last = wo_part(n, t, 4 + t)
                    if t == TT - 1 or n == N_UP - 1:
                        last.then_inc(pe_done, 1)

                def h2_transposes(t):
                    pe.wait_ge(normed, NORMED_H2 + t + 1)
                    for half in range(2):
                        b = 2 * (t % 2) + half
                        pe.wait_ge(taken[b], TAKEN_WO[b] + 1 + t // 2)
                        for c in range(4):
                            last = nc.tensor.transpose(bank[b][:, c * P:(c + 1) * P],
                                                       temp2[:, t % 2, (4 * half + c) * P:(4 * half + c + 1) * P],
                                                       ident[:, :])
                        last.then_inc(pe_done, 1)
                if t:
                    h2_transposes(t - 1)
            h2_transposes(TT - 1)

            for b in range(4):
                pe.wait_ge(taken[b], TAKEN_UP[b])
            def up_pair(i):
                for r in range(4):
                    n = N_UP + r
                    pe.wait_ge(lo_ready, i * 4 + n + 1)
                    pe.wait_ge(taken[4 + r], i + TAKEN_UP[4 + r])
                    feature_block(bank[4 + r], slot_of(n), a_in).then_inc(pe_done, 1)

            with pe.Fori(0, UP_IT - 1) as i:
                up_pair(i)
            up_pair(UP_IT - 1)

            def down_part(m, half, t, s, first, last_block):
                for k in range(2):
                    a = (m % 2 * 2 + k) * SEQ + t * P
                    last = matmul3(bank[4 * half + t][:, :], aring_hi[:, a:a + P], aring_lo[:, a:a + P],
                                   w_hi[:, s, k * 512:(k + 1) * 512], w_lo[:, s, k * 512:(k + 1) * 512],
                                   first and k == 0, last_block and k == 1)
                return last

            def down_pair(m, i, first):
                pe.wait_ge(ring_lo, i * 2 + m + 1)
                for half in range(2):
                    n = N_DN + 2 * m + half
                    pe.wait_ge(lo_ready, i * 4 + n + 1)
                    for t in range(TT):
                        if first:
                            pe.wait_ge(taken[4 * half + t], TAKEN_DN[4 * half + t])
                        last = down_part(m, half, t, slot_of(n), first, False)
                    last.then_inc(pe_done, 1)

            down_pair(0, 0, True)
            with pe.Fori(0, DN_IT) as i:
                down_pair(1, i, False)
                down_pair(2, i, False)
            down_pair(FB // 2 - 2, 0, False)
            pe.wait_ge(ring_lo, FB // 2)
            pe.wait_ge(lo_ready, N_END)
            for t in range(TT):
                for half in range(2):
                    down_part(FB // 2 - 1, half, t, slot_of(N_END - 2 + half), False, True).then_inc(pe_done, 1)

        @block.sync
        def _(sp):
            def load(n, src, width, i=0, period=0):
                if period and n != N_J + 6:
                    sp.wait_ge(lo_ready, i * period + previous(n + (n == N_J + 5)) + 1)
                elif period:
                    pass
                elif previous(n) is not None:
                    sp.wait_ge(lo_ready, previous(n) + 1)
                s = slot_of(n)
                sp.dma_start(stage[:, s, :].rearrange("p (k c) -> p k c", c=width), src).then_inc(w_loaded[s], 16)

            for t in range(MT):
                sp.dma_start(mem_t[:, t, :], mem_v[:, t, :]).then_inc(mem_in[t], 16)
            for n in range(N_MEMK, N_Q):
                r = n % 4
                load(n, wkv_v[:, 2 * r:2 * r + 2, (n // 4) * 512:(n // 4 + 1) * 512], 512)
                if n == 5:
                    sp.wait_ge(taken[BANK[("relvec",)]], NTH[("relvec",)])
                    sp.dma_start(rel_dram, rel_row).then_inc(relvec_out, 16)
                    sp.wait_ge(relvec_out, 16)
                    sp.wait_ge(pe_done, DONE[("memT", 1, 1)])
                    sp.dma_start(rel_flip, bass.AP(tensor=rel_dram.tensor, offset=0,
                                                   ap=[[1, P], [REL, NH], [1, WIN]])).then_inc(relflip_in, 16)
            for n in range(N_Q, N_CONV):
                if n < N_MQ2:
                    r, c0 = n % 4, ATT0 + (n - N_Q) // 4 * 512
                    load(n, win_v[:, 2 * r:2 * r + 2, c0:c0 + 512], 512)
                else:
                    r, c0 = n - N_MQ2, MQ0 + 256
                    load(n, win_v[:, 4 * r:4 * r + 4, c0:c0 + 256], 256)
            for n in range(N_CONV, N_J):
                r = n - N_CONV
                c0 = (CONV_W, 2 * CONV_W, 0)[r % 6 // 2] + (r // 6 * 2 + r % 2) * P
                load(n, win_v[:, :, c0:c0 + P], P)
            with sp.Fori(0, J_IT) as i:
                for r in range(J_WT):
                    if r < 6:
                        load(N_J + r, win_v[:, :, ds(i * 256 + (GATE0 + r // 2 * D + r % 2 * P), P)], P, i, J_WT)
                    else:
                        load(N_J + r, wbr_v[r - 6][:, :, ds(i * 256, 256)], 256, i, J_WT)
            sp.wait_ge(pe_done, DONE0 + J_DONE)
            sp.dma_start(x2, x_v).then_inc(x_again, 16)
            sp.dma_start(gain_ffn, norm_ffn.broadcast_to([P, D])).then_inc(ffn_gain_in, 16)
            for n in range(N_WO, N_UP):
                r = n - N_WO
                load(n, wo_v[:, r % 4 * 2:r % 4 * 2 + 2, r // 4 * 512:(r // 4 + 1) * 512], 512)
            with sp.Fori(0, UP_IT) as i:
                for r in range(4):
                    load(N_UP + r, wup_v[:, :, ds(i * 256 + (r % 2 * FF + r // 2 * P), P)], P, i, 4)
            with sp.Fori(0, FB // 4) as i:
                for r in range(4):
                    load(N_DN + r, wdn_v[:, ds(i * 4 + r // 2 * 2, 2), r % 2 * 512:(r % 2 + 1) * 512], 512, i, 4)
            for half in range(2):
                load(N_END - 2 + half, wdn_v[:, FB - 2:FB, half * 512:(half + 1) * 512], 512)
            for t in range(TT):
                sp.wait_ge(final, 2 * t + 2)
                sp.dma_start(out_v[:, t, :], x2[:, t, :]).then_inc(stored, 16)
            sp.wait_ge(stored, 16 * TT)

        @block.gpsimd
        def _(pool):
            count = [0]

            def inverse_root(v, width):
                count[0] += 1
                pool.wait_ge(var_ready, count[0])
                nc.gpsimd.tensor_tensor(v, v, neg_half[:, 0:width], ALU.pow).then_inc(pow_ready, 1)

            nc.gpsimd.memset(neg_half, -0.5).then_inc(zeroed, 1)
            pool.wait_ge(zeroed, 1)
            for t in range(MT + TT):
                inverse_root(ss[:, t:t + 1], 1)
            pool.wait_ge(relvec_out, 16)
            for t in range(MT):
                wait_taken(pool, ("mk", t))
                nc.gpsimd.tensor_tensor(temp[:, t, :], mk_raw[:, t, :], mk_raw[:, t, :], ALU.mult).then_inc(sq_ready, 1)
            for t in range(MT):
                inverse_root(mk_[:, t, :], MH)
            for t in range(TT):
                wait_taken(pool, ("q", t))
                if t == 0:
                    pool.wait_ge(pe_done, DONE[("bias", 3)])
                nc.gpsimd.tensor_tensor(temp[:, t, :], raw_a[:, t, :], raw_a[:, t, :], ALU.mult).then_inc(sq_ready, 1)
            for t in range(TT):
                inverse_root(hv[:, t, :], NH)
            for t in range(TT):
                wait_taken(pool, ("kvm", t))
                nc.gpsimd.tensor_tensor(temp[:, t, :], raw_b[:, t, :], raw_b[:, t, :], ALU.mult).then_inc(sq_ready, 1)
                nc.gpsimd.tensor_copy(v_t[:, t, :], raw_b[:, t, P:2 * P]).then_inc(v_ready, 1)
            for t in range(TT):
                inverse_root(kv_[:, t, :], 4)
            for t in range(TT):
                wait_taken(pool, ("mq2", t))
                nc.gpsimd.tensor_tensor(temp[:, t, 256:512], raw_a[:, t, 0:256], raw_a[:, t, 0:256],
                                        ALU.mult).then_inc(sq_ready, 1)
            for t in range(TT):
                inverse_root(mq_[:, t, 0:2], 2)
            pool.wait_ge(pe_done, DONE[("kmT", TT - 1)])
            nc.gpsimd.memset(probs[:, :, 0:CHUNK], 0.0).then_inc(zeroed, 1)
            pool.wait_ge(zeroed, 2)

            def normalise(t):
                lo = 0 if t else CHUNK
                pool.wait_ge(recip, t + 1)
                p = probs[:, :, CHUNK + lo:256]
                nc.gpsimd.tensor_tensor(p, p, den[:, :].unsqueeze(2).broadcast_to([P, NH, WIN - lo]),
                                        ALU.mult).then_inc(probs_ready, 1)

            def mem_normalise(t):
                pool.wait_ge(mrecip, t + 1)
                nc.gpsimd.tensor_tensor(mprobs, mprobs, mden[:, :].unsqueeze(2).broadcast_to([P, MH, MEM]),
                                        ALU.mult).then_inc(mprobs_ready, 1)

            for t in range(TT):
                normalise(t)
                mem_normalise(t)
            for t in range(TT):
                inverse_root(ss[:, t:t + 1], 1)

        @block.scalar
        def _(act_):
            def split_hi(n, i=0, period=0):
                s = slot_of(n)
                if period:
                    act_.wait_ge(w_loaded[s], line(lambda m: 16 * uses(m), n, i, period))
                    act_.wait_ge(pe_done, line(lambda m: used(previous(m)), n, i, period))
                else:
                    act_.wait_ge(w_loaded[s], 16 * uses(n))
                    if previous(n) is not None:
                        act_.wait_ge(pe_done, used(previous(n)))
                nc.scalar.activation(w_hi[:, s, :], stage[:, s, :], ACT.Copy).then_inc(hi_ready, 1)

            def take(name, dst, scale=None, columns=slice(0, 512), frees=True):
                act_.wait_ge(pe_done, DONE[name])
                src = bank[BANK[name]][:, columns]
                if len(dst.shape) == 3:
                    src = src.rearrange("p (a c) -> p a c", a=dst.shape[1])
                if len(dst.shape) == 4:
                    src = src.rearrange("p (a b c) -> p a b c", a=dst.shape[1], b=dst.shape[2])
                ins = nc.scalar.activation(dst, src, ACT.Copy, scale=1.0 if scale is None else scale)
                ins.then_inc(taken[BANK[name]] if frees else hi_taken, 1)

            act_.dma_start(gain_mem, norm_mem.broadcast_to([P, D])).then_inc(gains_in, 16)
            act_.dma_start(ident[:, :], eye).then_inc(eye_in, 16)
            for t in range(TT):
                act_.dma_start(x_t[:, t, :], x_v[:, t, :]).then_inc(x_in[t], 16)
            act_.dma_start(gain_mix, norm_mix.broadcast_to([P, D])).then_inc(gains_in, 16)
            for ins in (
                act_.dma_start(params[0:24, 0, :], b_gate[0].rearrange("(b c) -> b c", c=P)),
                act_.dma_start(params[24:36, 0, :], conv_w[0].rearrange("a (b c) -> (a b) c", c=P)),
                act_.dma_start(params[36:37, 0, 0:HD], q_norm),
                act_.dma_start(params[36:37, 0, HD:P], q_norm),
                act_.dma_start(params[37:38, 0, 0:HD], k_norm),
                act_.dma_start(params[37:38, 0, HD:P], k_norm),
                act_.dma_start(params[38:39, 0, :], mq_norm),
                act_.dma_start(params[39:40, 0, :], mk_norm),
                act_.dma_start(params[40:84, 0, :], ffn_conv_b[0].rearrange("(b c) -> b c", c=P)),
                act_.dma_start(params[0:88, 1, :], ffn_conv_w[0, 0:2, :].rearrange("a (b c) -> (a b) c", c=P)),
                act_.dma_start(params[0:44, 2, :], ffn_conv_w[0, 2, :].rearrange("(b c) -> b c", c=P)),
            ):
                ins.then_inc(params_in, 16)
            act_.dma_start(rel_sb, rel_bias).then_inc(rel_in, 16)
            act_.dma_start(onehot, bucket_of).then_inc(rel_in, 16)
            act_.dma_start(flip_sb, flip).then_inc(rel_in, 16)
            act_.dma_start(sink, sinks.broadcast_to([P, NH])).then_inc(sink_in, 16)

            squared = [0]

            def square(src, junk, total):
                if squared[0]:
                    act_.wait_ge(squares, squared[0])
                squared[0] += 1
                nc.scalar.activation(junk, src, ACT.Square, accum_out=total).then_inc(squares, 1)

            junk = arena[:, 4096:5120]
            for t in range(MT):
                act_.wait_ge(mem_in[t], 16)
                square(mem_t[:, t, :], junk, ss[:, t:t + 1])
            split_hi(0)
            split_hi(1)
            for t in range(MT):
                for half in range(2):
                    take(("memT", t, half), memT_hi[:, 4 * half:4 * half + 4, t * P:(t + 1) * P], frees=False)

            def x_squares(t):
                act_.wait_ge(x_in[t], 16)
                square(x_t[:, t, :], junk, ss[:, MT + t:MT + t + 1])

            def x_hi(t):
                for half in range(2):
                    take(("xT", t, half), h_hi[:, 4 * half:4 * half + 4, t * P:(t + 1) * P], frees=False)

            for n in range(N_MEMK, N_Q):
                split_hi(n + 2)
                if n < 2:
                    x_squares(2 * n)
                    x_squares(2 * n + 1)
                if n == 3:
                    for t in range(MT):
                        take(("mk", t), mk_raw[:, t, :])
                if 2 <= n < 6:
                    x_hi(n - 2)
                if n == 6:
                    act_.wait_ge(params_done, 1)
                    for t in range(MT):
                        take(("mkT", t), mkT[:, :, t * P:(t + 1) * P], mkg)
                if n == 7:
                    for t in range(MT):
                        take(("mv", t), m_v[:, t, :])

            def raws(name, dst, width):
                for t in range(TT):
                    take((name, t), dst[:, t, 0:width], columns=slice(0, width))

            def heads(ap, a):
                return ap.rearrange("p (a c) -> p a c", a=a)

            def keys(t):
                act_.wait_ge(pe_done, DONE[("kmT", t)])
                nc.scalar.activation(kT[:, :, t * P:(t + 1) * P], heads(bank[BANK[("kmT", t)]][:, 0:256], NKV),
                                     ACT.Copy, scale=kg)
                take(("kmT", t), mqT[:, 0:2, t * P:(t + 1) * P], mqg, columns=slice(256, 512))

            def exps(t):
                lo = 0 if t else CHUNK
                act_.wait_ge(maxed, t + 1)
                for hh in range(NH):
                    p = probs[:, hh, CHUNK + lo:256]
                    nc.scalar.activation(p, p, ACT.Exp, bias=top[:, hh:hh + 1], accum_out=den[:, hh:hh + 1])
                nc.scalar.activation(sink_e, sink_e, ACT.Exp).then_inc(expd, 1)

            def mem_exps(t):
                act_.wait_ge(mmaxed, t + 1)
                if t:
                    act_.wait_ge(pe_done, DONE[("mprobT", t - 1, 1)])
                for hh in range(MH):
                    ins = nc.scalar.activation(mprobs[:, hh, :], bank[BANK[("mscore", t, hh // 2)]]
                                               [:, hh % 2 * MEM:(hh % 2 + 1) * MEM], ACT.Exp,
                                               bias=mtop[:, hh:hh + 1], accum_out=mden[:, hh:hh + 1])
                    if hh % 2:
                        ins.then_inc(taken[BANK[("mscore", t, hh // 2)]], 1)

            def attend(t):
                for kt in ((0, 1) if t else (1,)):
                    take(("probT", t, kt, 0), probT[:, kt, 0, :, :].rearrange("p r c -> p (r c)"))
                take(("attn", t), a_hi[:, 4:8, t * P:(t + 1) * P], frees=False)

            def mem_attend(t):
                take(("mprobT", t, 0), mprobT[:, 0, :])
                take(("mattn", t), a_hi[:, 8:12, t * P:(t + 1) * P], frees=False)

            for n in range(N_Q, N_CONV):
                split_hi(n + 2)
                if n in (13, 14):
                    for t in (2 * (n - 13), 2 * (n - 13) + 1):
                        take(("qT", t), qT[:, :, t * P:(t + 1) * P], qg)
                if n == N_KVM - 1:
                    raws("q", raw_a, 512)
                if n == N_MQ2 - 1:
                    raws("kvm", raw_b, 512)
                if n == 16:
                    keys(0)
                    keys(1)
                if n == N_CONV - 1:
                    raws("mq2", raw_a, 256)
                    keys(2)
                    keys(3)
            for n in range(N_CONV, N_J):
                split_hi(n + 2)
                r, pair = (n - N_CONV) % 6, (n - N_CONV) // 6
                if n == 18:
                    exps(0)
                if n - 1 in MEM_SCORES:
                    mem_exps(MEM_SCORES.index(n - 1))
                if n - 1 in ATTEND:
                    exps(ATTEND.index(n - 1) + 1)
                if r < 2:
                    if pair:
                        act_.wait_ge(conv_x, r + 1)
                    take(("conv", n), temp[:, r, :])
                if n == 18:
                    for a in range(2):
                        take(("mq2T", a), mqT[:, 2:4, 2 * a * P:2 * (a + 1) * P].rearrange("p h (t c) -> p t h c", t=2),
                             mqg)
                if r >= 4:
                    c = 2 * pair + r - 4
                    wait_taken(act_, ("conv", n))
                    nc.scalar.activation(a_hi[:, c, :], temp[:, 2 + c % 2, :], ACT.Copy).then_inc(conv_hi, 1)
                if n in ATTEND:
                    attend(ATTEND.index(n))
                if n in MEM_ATTEND:
                    mem_attend(MEM_ATTEND.index(n))

            def merge_pair(i, last):
                for r in range(J_WT):
                    split_hi(N_J + r + 2, i, J_WT) if not last else split_hi(N_J + (J_IT - 1) * J_WT + r + 2)
                    if r < 6:
                        act_.wait_ge(pe_done, i * J_DONE + DONE0 + r + 1)
                        nc.scalar.activation(sig[:, r, :], bank[r % 4][:, :], ACT.Sigmoid,
                                             bias=bg_col[:, ds(i * 2 + (r // 2 * KD + r % 2), 1)])\
                            .then_inc(taken[r % 4], 1)
                    if last and r in (6, 7):
                        for j in range(3 * (r - 6), 3 * (r - 5)):
                            merged_split(j)

            def merged_split(j):
                if j == 0:
                    act_.wait_ge(pe_done, DONE0 + J_DONE * (J_IT - 1) + 6)
                if j % 2 == 0:
                    act_.wait_ge(merged_ready, j + 2)
                nc.scalar.activation(h_hi[:, j, :], merged[:, j * SEQ:(j + 1) * SEQ], ACT.Copy).then_inc(merged_hi, 1)

            with act_.Fori(0, J_IT - 1) as i:
                merge_pair(i, False)
                act_.wait_ge(taken[7], i + TAKEN0[7] + 1)
            merge_pair(J_IT - 1, True)
            merged_split(6)
            merged_split(7)

            def x2_squares(t, half, total):
                b = t + 4 * half
                act_.wait_ge(taken[b], TAKEN_WO[b] + 1)
                square(x2[:, t, half * 512:(half + 1) * 512], arena[:, 8192:8704], total[:, t:t + 1])

            def h2_hi(t):
                for half in range(2):
                    act_.wait_ge(pe_done, WO_AT[("h2T", t)] - 1 + half)
                    nc.scalar.activation(a_hi[:, 4 * half:4 * half + 4, t * P:(t + 1) * P],
                                         bank[2 * (t % 2) + half][:, :].rearrange("p (a c) -> p a c", a=4), ACT.Copy)\
                        .then_inc(hi_taken, 1)

            for n in range(N_WO + 2, N_WO + 8):
                split_hi(n)
            for t in range(TT):
                x2_squares(t, 0, ss2a)
            for t in range(TT):
                if t == TT - 1:
                    split_hi(N_UP)
                    split_hi(N_UP + 1)
                x2_squares(t, 1, ss2b)
                if t:
                    h2_hi(t - 1)
            h2_hi(TT - 1)

            def ring(m, i=0, wait=None):
                if wait is not None:
                    act_.wait_ge(pe_done, wait)
                nc.scalar.activation(aring_hi[:, m % 2 * 1024:(m % 2 + 1) * 1024],
                                     act[:, ds(i * 2048 + m * 1024, 1024)], ACT.Copy).then_inc(ring_hi, 1)

            def up_pair(i, last):
                for r in range(4):
                    if last:
                        split_hi(N_UP + 4 * (UP_IT - 1) + r + 2)
                    else:
                        split_hi(N_UP + r + 2, i, 4)
                    if r % 2:
                        act_.wait_ge(taken[3 + r], i + TAKEN_UP[3 + r] + 1)
                        nc.scalar.activation(temp[:, r - 1, :], temp[:, r - 1, :], ACT.Silu).then_inc(silu_ready, 1)
                    col = i * 2 + (r % 2 * FB + r // 2)
                    act_.wait_ge(pe_done, i * UP_DONE + DONE_UP + r + 1)
                    nc.scalar.activation(temp[:, r, :], bank[4 + r][:, :], ACT.Identity,
                                         bias=fb_col[:, ds(col, 1)], scale=fw_col[:, ds(col + 4 * FB, 1)])\
                        .then_inc(tap_ready, 1)

            with act_.Fori(0, UP_IT - 1) as i:
                up_pair(i, False)
                act_.wait_ge(act_ready, i * 2 + 2)
            act_.wait_ge(act_ready, 2)
            ring(0)
            up_pair(UP_IT - 1, True)

            ring(1)
            split_hi(N_DN + 2)
            split_hi(N_DN + 3)

            def down_pair(m, i):
                ring(m + 1, i, i * 4 + DONE_DN + 2 * m)
                split_hi(N_DN + 2 * m + 2, i, 4)
                split_hi(N_DN + 2 * m + 3, i, 4)

            with act_.Fori(0, DN_IT) as i:
                down_pair(1, i)
                down_pair(2, i)
            act_.wait_ge(act_ready, FB)
            m = FB // 2 - 2
            ring(m + 1, 0, DONE_DN + 2 * m)
            split_hi(N_END - 2)
            split_hi(N_END - 1)

        @block.vector
        def _(dve):
            chain = [0]

            def then(ins, base=0):
                chain[0] += 1
                ins.then_inc(dve_chain, 1)
                dve.wait_ge(dve_chain, base + chain[0])

            def split_lo(n, i=0, period=0):
                s = slot_of(n)
                dve.wait_ge(hi_ready, i * period + n + 1)
                nc.vector.tensor_tensor(w_lo[:, s, :], stage[:, s, :], w_hi[:, s, :].bitcast(f32),
                                        ALU.subtract).then_inc(lo_ready, 1)

            hi_parts = [0]

            def take_lo(name, hi, lo):
                hi_parts[0] += 1
                dve.wait_ge(hi_taken, hi_parts[0])
                nc.vector.tensor_tensor(lo, bank[BANK[name]][:, :].rearrange("p (a c) -> p a c", a=4),
                                        hi.bitcast(f32), ALU.subtract).then_inc(taken[BANK[name]], 1)

            def variance(v, parts):
                for k, (c0, c1, width) in enumerate(parts):
                    ins = nc.vector.tensor_scalar(v[:, c0:c1], v[:, c0:c1], 1.0 / width, EPS, ALU.mult, ALU.add)
                    if k == len(parts) - 1:
                        ins.then_inc(var_ready, 1)

            powed = [0]

            def wait_pow():
                powed[0] += 1
                dve.wait_ge(pow_ready, powed[0])

            def row_norm(tile, v, gain):
                wait_pow()
                nc.vector.scalar_tensor_tensor(out=tile, in0=tile, scalar=v, in1=gain, op0=ALU.mult,
                                               op1=ALU.mult).then_inc(normed, 1)

            def head_norm(dst, src, v, shape, signal=True):
                a, w = shape
                ins = nc.vector.tensor_tensor(dst, src, v.unsqueeze(2).broadcast_to([P, a, w]), ALU.mult)
                if signal:
                    ins.then_inc(normed, 1)
                return ins

            def heads(ap, a):
                return ap.rearrange("p (a c) -> p a c", a=a)

            for t in range(MT):
                dve.wait_ge(squares, t + 1)
                variance(ss, [(t, t + 1, D)])
            for t in range(MT):
                if t == 0:
                    dve.wait_ge(gains_in, 32)
                row_norm(mem_t[:, t, :], ss[:, t:t + 1], gain_mem)
            split_lo(0)
            split_lo(1)
            for t in range(MT):
                for half in range(2):
                    at = (slice(None), slice(4 * half, 4 * half + 4), slice(t * P, (t + 1) * P))
                    take_lo(("memT", t, half), memT_hi[at], memT_lo[at])

            for n in range(N_MEMK, N_Q):
                split_lo(n + 2)
                if n < 2:
                    for t in (2 * n, 2 * n + 1):
                        dve.wait_ge(squares, MT + t + 1)
                        variance(ss, [(MT + t, MT + t + 1, D)])
                    for t in (2 * n, 2 * n + 1):
                        row_norm(x_t[:, t, :], ss[:, MT + t:MT + t + 1], gain_mix)
                if n == 1:
                    dve.wait_ge(pe_done, DONE[("params",)])
                    nc.vector.tensor_copy(cols[:, :], bank[BANK[("params",)]][:, 0:216])\
                        .then_inc(taken[BANK[("params",)]], 1)
                    wait_taken(dve, ("params",))
                    nc.vector.tensor_scalar(qg, qg, HD ** -0.5, None, ALU.mult)
                    nc.vector.tensor_scalar(mqg, mqg, MHD ** -0.5, None, ALU.mult).then_inc(params_done, 1)
                    dve.wait_ge(pe_done, DONE[("relvec",)])
                    nc.vector.tensor_copy(rel_row, bank[BANK[("relvec",)]][0:NH, 0:REL])\
                        .then_inc(taken[BANK[("relvec",)]], 1)
                if n == 3:
                    for t in range(MT):
                        dve.wait_ge(sq_ready, t + 1)
                        then(nc.vector.tensor_reduce(out=mk_[:, t, :], in_=heads(temp[:, t, :], MH), op=ALU.add,
                                                     axis=AX.X))
                        variance(mk_[:, t, :], [(0, MH, MHD)])
                if n == 4:
                    for t in range(MT):
                        wait_pow()
                        head_norm(heads(mk_raw[:, t, :], MH), heads(mk_raw[:, t, :], MH), mk_[:, t, :], (MH, MHD))
                if 2 <= n < 6:
                    t = n - 2
                    for half in range(2):
                        at = (slice(None), slice(4 * half, 4 * half + 4), slice(t * P, (t + 1) * P))
                        take_lo(("xT", t, half), h_hi[at], h_lo[at])

            for n in range(N_Q, N_CONV):
                split_lo(n + 2)
                if n == 10:
                    for a in range(4):
                        name = ("bias", a)
                        dve.wait_ge(pe_done, DONE[name])
                        nc.vector.tensor_copy(bias[:, 2 * a:2 * a + 2, :], heads(bank[BANK[name]][:, 0:2 * WIN], 2))\
                            .then_inc(taken[BANK[name]], 1)
                    dve.wait_ge(taken[BANK[("bias", 3)]], NTH[("bias", 3)])
                    nc.vector.memset(bias[0:CHUNK, :, 2 * CHUNK:WIN], MASKED)
                    then(nc.vector.memset(bias[CHUNK:P, :, 0:CHUNK], MASKED))
                if n == N_KVM - 1:
                    for t in range(TT):
                        dve.wait_ge(sq_ready, MT + t + 1)
                        then(nc.vector.tensor_reduce(out=hv[:, t, :], in_=heads(temp[:, t, :], NH), op=ALU.add,
                                                     axis=AX.X))
                        variance(hv[:, t, :], [(0, NH, HD)])
                    for t in range(TT):
                        wait_pow()
                        head_norm(heads(raw_a[:, t, :], NH), heads(raw_a[:, t, :], NH), hv[:, t, :], (NH, HD))
                if n == N_MQ2 - 1:
                    for t in range(TT):
                        dve.wait_ge(sq_ready, MT + TT + t + 1)
                        nc.vector.tensor_reduce(out=kv_[:, t, 0:2], in_=heads(temp[:, t, 0:P], 2), op=ALU.add, axis=AX.X)
                        then(nc.vector.tensor_reduce(out=kv_[:, t, 2:4], in_=heads(temp[:, t, 256:512], 2), op=ALU.add,
                                                     axis=AX.X))
                        variance(kv_[:, t, :], [(0, 2, HD), (2, 4, MHD)])
                    for t in range(TT):
                        wait_pow()
                        for g in range(NKV):
                            nc.vector.tensor_tensor(
                                temp[:, t, g * P:(g + 1) * P].rearrange("p (a c) -> p a c", a=2),
                                raw_b[:, t, g * HD:(g + 1) * HD].unsqueeze(1).broadcast_to([P, 2, HD]),
                                kv_[:, t, g:g + 1].unsqueeze(2).broadcast_to([P, 2, HD]), ALU.mult)
                        head_norm(heads(raw_b[:, t, 256:512], 2), heads(raw_b[:, t, 256:512], 2), kv_[:, t, 2:4],
                                  (2, MHD))
                if n == N_CONV - 1:
                    for t in range(TT):
                        dve.wait_ge(sq_ready, MT + 2 * TT + t + 1)
                        then(nc.vector.tensor_reduce(out=mq_[:, t, 0:2], in_=heads(temp[:, t, 256:512], 2), op=ALU.add,
                                                     axis=AX.X))
                        variance(mq_[:, t, 0:2], [(0, 2, MHD)])
                    for t in range(TT):
                        wait_pow()
                        head_norm(heads(raw_a[:, t, 0:256], 2), heads(raw_a[:, t, 0:256], 2), mq_[:, t, 0:2], (2, MHD))

            def tops(t):
                lo = 0 if t else CHUNK
                dve.wait_ge(zeroed, 2)
                if t:
                    dve.wait_ge(pe_done, DONE[("probT", t - 1, 1, 1)])
                else:
                    dve.wait_ge(sink_in, 16)
                for g in range(NKV):
                    for r in range(2):
                        name = ("score", t, g, r)
                        dve.wait_ge(pe_done, DONE[name])
                        nc.vector.tensor_tensor(probs[:, 4 * g + r:4 * g + r + 3:2, CHUNK + lo:256],
                                                heads(bank[BANK[name]][:, 0:2 * WIN], 2)[:, :, lo:WIN],
                                                bias[:, 4 * g + r:4 * g + r + 3:2, lo:WIN], ALU.add)\
                            .then_inc(taken[BANK[name]], 1)
                for g in range(NKV):
                    for r in range(2):
                        name = ("score", t, g, r)
                        dve.wait_ge(taken[BANK[name]], NTH[name])
                then(nc.vector.tensor_reduce(out=top, in_=probs[:, :, CHUNK + lo:256], op=ALU.max, axis=AX.X))
                then(nc.vector.tensor_tensor(top, top, sink, ALU.max))
                then(nc.vector.tensor_scalar(top, top, -1.0, None, ALU.mult))
                nc.vector.tensor_tensor(sink_e, sink, top, ALU.add).then_inc(maxed, 1)

            def sums(t):
                dve.wait_ge(expd, t + 1)
                then(nc.vector.tensor_tensor(den, den, sink_e, ALU.add))
                nc.vector.reciprocal(den, den).then_inc(recip, 1)

            def mem_tops(t):
                for a in range(2):
                    dve.wait_ge(pe_done, DONE[("mscore", t, a)])
                    ins = nc.vector.tensor_reduce(out=mtop[:, 2 * a:2 * a + 2],
                                                  in_=heads(bank[BANK[("mscore", t, a)]][:, :], 2), op=ALU.max, axis=AX.X)
                then(ins)
                nc.vector.tensor_scalar(mtop, mtop, -1.0, None, ALU.mult).then_inc(mmaxed, 1)

            def mem_sums(t):
                for a in range(2):
                    wait_taken(dve, ("mscore", t, a))
                nc.vector.reciprocal(mden, mden).then_inc(mrecip, 1)

            def attend(t):
                for kt in ((0, 1) if t else (1,)):
                    name = ("probT", t, kt, 1)
                    dve.wait_ge(pe_done, DONE[name])
                    nc.vector.tensor_copy(probT[:, kt, 1, :, :].rearrange("p r c -> p (r c)"), bank[BANK[name]][:, :])\
                        .then_inc(taken[BANK[name]], 1)
                at = (slice(None), slice(4, 8), slice(t * P, (t + 1) * P))
                take_lo(("attn", t), a_hi[at], a_lo[at])

            def mem_attend(t):
                name = ("mprobT", t, 1)
                dve.wait_ge(pe_done, DONE[name])
                nc.vector.tensor_copy(mprobT[:, 1, :], bank[BANK[name]][:, :]).then_inc(taken[BANK[name]], 1)
                at = (slice(None), slice(8, 12), slice(t * P, (t + 1) * P))
                take_lo(("mattn", t), a_hi[at], a_lo[at])

            tops(0)
            for n in range(N_CONV, N_J):
                split_lo(n + 2)
                r, pair = (n - N_CONV) % 6, (n - N_CONV) // 6
                name = ("conv", n)
                if n - 1 in MEM_SCORES:
                    mem_tops(MEM_SCORES.index(n - 1))
                if r in (2, 3):
                    c, k = 2 * pair + r - 2, r - 2
                    wait_taken(dve, ("conv", n - 2))
                    dve.wait_ge(pe_done, DONE[name])
                    nc.vector.tensor_tensor(temp[:, k, :], bank[BANK[name]][:, :], temp[:, k, :], ALU.mult)\
                        .then_inc(taken[BANK[name]], 1)
                    dve.wait_ge(taken[BANK[name]], NTH[name])
                    w = [cw_col[:, a * CB + c:a * CB + c + 1] for a in range(3)]
                    then(nc.vector.tensor_scalar(temp[:, 2 + k, :], temp[:, k, :], w[2], None, ALU.mult))
                    then(nc.vector.scalar_tensor_tensor(out=temp[:, 2 + k, 1:SEQ], in0=temp[:, k, 0:SEQ - 1], scalar=w[1],
                                                        in1=temp[:, 2 + k, 1:SEQ], op0=ALU.mult, op1=ALU.add))
                    nc.vector.scalar_tensor_tensor(out=temp[:, 2 + k, 2:SEQ], in0=temp[:, k, 0:SEQ - 2], scalar=w[0],
                                                   in1=temp[:, 2 + k, 2:SEQ], op0=ALU.mult, op1=ALU.add)\
                        .then_inc(conv_x, 1)
                if r >= 4:
                    c, k = 2 * pair + r - 4, r - 4
                    dve.wait_ge(pe_done, DONE[name])
                    dve.wait_ge(conv_x, c + 1)
                    nc.vector.tensor_tensor(temp[:, 2 + k, :], bank[BANK[name]][:, :], temp[:, 2 + k, :], ALU.mult)\
                        .then_inc(taken[BANK[name]], 1)
                    dve.wait_ge(conv_hi, c + 1)
                    nc.vector.tensor_tensor(a_lo[:, c, :], temp[:, 2 + k, :], a_hi[:, c, :].bitcast(f32),
                                            ALU.subtract).then_inc(conv_lo, 1)
                if n == 18:
                    sums(0)
                if n - 1 in ATTEND:
                    sums(ATTEND.index(n - 1) + 1)
                if n - 1 in MEM_SCORES:
                    mem_sums(MEM_SCORES.index(n - 1))
                if n in ATTEND:
                    attend(ATTEND.index(n))
                    if n != ATTEND[-1]:
                        tops(ATTEND.index(n) + 1)
                if n in MEM_ATTEND:
                    mem_attend(MEM_ATTEND.index(n))

            def merge_pair(i, base, last):
                for r in range(J_WT):
                    if last:
                        split_lo(N_J + (J_IT - 1) * J_WT + r + 2)
                    else:
                        split_lo(N_J + r + 2, i, J_WT)
                    for jj in range(2) if r >= 6 else ():
                        b = 2 + 2 * (r - 6) + jj
                        gate_b = (2 * (r - 6) + jj) % 4
                        dve.wait_ge(taken[gate_b], i * J_TAKEN[gate_b] + TAKEN0[gate_b] + (2 if r == 8 else 1))
                        dve.wait_ge(pe_done, i * J_DONE + DONE0 + 6 + 2 * (r - 6) + jj + 1)
                        m = merged[:, ds(i * 1024 + jj * SEQ, SEQ)]
                        g = sig[:, 2 * (r - 6) + jj, :]
                        if r == 6:
                            nc.vector.tensor_tensor(m, bank[b][:, :], g, ALU.mult).then_inc(taken[b], 1)
                            continue
                        nc.vector.tensor_tensor(merge_tmp[:, jj, :], bank[b][:, :], g, ALU.mult).then_inc(taken[b], 1)
                        dve.wait_ge(taken[b], i * J_TAKEN[b] + TAKEN0[b] + 1)
                        if r == 7:
                            dve.wait_ge(taken[2 + jj], i * J_TAKEN[2] + TAKEN0[2 + jj] + 2)
                            then(nc.vector.tensor_tensor(m, m, merge_tmp[:, jj, :], ALU.add), base)
                        else:
                            nc.vector.tensor_tensor(m, m, merge_tmp[:, jj, :], ALU.add).then_inc(merged_ready, 1)
                    if last and r in (7, 8):
                        for j in range(3 * (r - 7), 3 * (r - 6)):
                            merged_split(j)

            def merged_split(j):
                dve.wait_ge(merged_hi, j + 1)
                nc.vector.tensor_tensor(h_lo[:, j, :], merged[:, j * SEQ:(j + 1) * SEQ], h_hi[:, j, :].bitcast(f32),
                                        ALU.subtract).then_inc(merged_lo, 1)

            with dve.Fori(0, J_IT - 1) as i:
                merge_pair(i, i * 2, False)
            chain[0] += 2 * (J_IT - 2)
            merge_pair(J_IT - 1, 0, True)
            merged_split(6)
            merged_split(7)

            for n in range(N_WO + 2, N_WO + 8):
                split_lo(n)
            dve.wait_ge(x_again, 16)
            dve.wait_ge(ffn_gain_in, 16)

            def add_x2(t, half):
                b = t + 4 * half
                dve.wait_ge(pe_done, WO_AT[("wo", t)] if half else DONE_WO + 4 + t)
                x2_half = x2[:, t, half * 512:(half + 1) * 512]
                nc.vector.tensor_tensor(x2_half, bank[b][:, :], x2_half, ALU.add).then_inc(taken[b], 1)

            def h2_norm(t):
                dve.wait_ge(squares, MT + TT + TT + t + 1)
                then(nc.vector.tensor_tensor(ss2a[:, t:t + 1], ss2a[:, t:t + 1], ss2b[:, t:t + 1], ALU.add))
                variance(ss2a[:, t:t + 1], [(0, 1, D)])
                wait_pow()
                if t >= 2:
                    dve.wait_ge(pe_done, WO_AT[("h2T", t - 2)])
                nc.vector.scalar_tensor_tensor(out=temp2[:, t % 2, :], in0=x2[:, t, :], scalar=ss2a[:, t:t + 1],
                                               in1=gain_ffn, op0=ALU.mult, op1=ALU.mult).then_inc(normed, 1)

            def h2_lo(t):
                for half in range(2):
                    hi_parts[0] += 1
                    dve.wait_ge(hi_taken, hi_parts[0])
                    b = 2 * (t % 2) + half
                    at = (slice(None), slice(4 * half, 4 * half + 4), slice(t * P, (t + 1) * P))
                    nc.vector.tensor_tensor(a_lo[at], bank[b][:, :].rearrange("p (a c) -> p a c", a=4),
                                            a_hi[at].bitcast(f32), ALU.subtract).then_inc(taken[b], 1)

            for t in range(TT):
                add_x2(t, 0)
            for t in range(TT):
                if t == TT - 1:
                    split_lo(N_UP)
                    split_lo(N_UP + 1)
                add_x2(t, 1)
                h2_norm(t)
                if t:
                    h2_lo(t - 1)
            h2_lo(TT - 1)

            def ring(m, i=0):
                dve.wait_ge(ring_hi, i * 2 + m + 1)
                part = slice(m % 2 * 1024, (m % 2 + 1) * 1024)
                nc.vector.tensor_tensor(aring_lo[:, part], act[:, ds(i * 2048 + m * 1024, 1024)],
                                        aring_hi[:, part].bitcast(f32), ALU.subtract).then_inc(ring_lo, 1)

            def up_pair(i, base, last):
                for r in range(4):
                    if last:
                        split_lo(N_UP + 4 * (UP_IT - 1) + r + 2)
                    else:
                        split_lo(N_UP + r + 2, i, 4)
                    b, u = 4 + r, temp[:, r, :]
                    col = i * 2 + (r % 2 * FB + r // 2)
                    dve.wait_ge(tap_ready, i * 4 + r + 1)
                    then(nc.vector.scalar_tensor_tensor(out=u[:, 1:SEQ], in0=bank[b][:, 0:SEQ - 1],
                                                        scalar=fw_col[:, ds(col + 2 * FB, 1)], in1=u[:, 1:SEQ],
                                                        op0=ALU.mult, op1=ALU.add), base)
                    nc.vector.scalar_tensor_tensor(out=u[:, 2:SEQ], in0=bank[b][:, 0:SEQ - 2],
                                                   scalar=fw_col[:, ds(col, 1)], in1=u[:, 2:SEQ],
                                                   op0=ALU.mult, op1=ALU.add).then_inc(taken[b], 1)
                    if r % 2:
                        dve.wait_ge(taken[b], i + TAKEN_UP[b] + 1)
                        dve.wait_ge(silu_ready, i * 2 + r // 2 + 1)
                        nc.vector.tensor_tensor(act[:, ds(i * 1024 + r // 2 * SEQ, SEQ)], temp[:, r - 1, :], u,
                                                ALU.mult).then_inc(act_ready, 1)

            with dve.Fori(0, UP_IT - 1) as i:
                up_pair(i, i * 4, False)
            chain[0] += 4 * (UP_IT - 2)
            ring(0)
            up_pair(UP_IT - 1, 0, True)

            ring(1)
            split_lo(N_DN + 2)
            split_lo(N_DN + 3)

            def down_pair(m, i):
                ring(m + 1, i)
                split_lo(N_DN + 2 * m + 2, i, 4)
                split_lo(N_DN + 2 * m + 3, i, 4)

            with dve.Fori(0, DN_IT) as i:
                down_pair(1, i)
                down_pair(2, i)
            ring(FB // 2 - 1)
            split_lo(N_END - 2)
            split_lo(N_END - 1)

            for t in range(TT):
                for half in range(2):
                    dve.wait_ge(pe_done, DONE_DN + FB - 2 + 2 * t + half + 1)
                    x2_half = x2[:, t, half * 512:(half + 1) * 512]
                    nc.vector.tensor_tensor(x2_half, bank[t + 4 * half][:, :], x2_half, ALU.add).then_inc(final, 1)


INPUTS = ["x", "mem", "rel_bias", "norm_mix", "norm_mem", "norm_ffn", "w_in", "b_gate", "conv_w", "q_norm", "k_norm",
          "sinks", "mq_norm", "mk_norm", "w_mem_kv", "w_br_conv", "w_br_attn", "w_br_mem", "w_o", "w_up",
          "ffn_conv_w", "ffn_conv_b", "w_down"]


def shape_constants():
    import numpy as np

    rel = np.arange(REL) - (P - 1) - CHUNK
    buckets, max_distance = 32, 128
    nb = buckets // 2
    n, exact = np.abs(rel), nb // 2
    large = exact + (np.log(np.maximum(n, 1) / exact) / np.log(max_distance / exact) * (nb - exact)).astype(np.int32)
    bucket = (rel > 0) * nb + np.where(n < exact, n, np.minimum(large, nb - 1))
    one = (np.arange(buckets)[:, None] == bucket[None, :]).astype(np.float32)
    eye = np.eye(P, dtype=np.float32)
    return {"eye": eye, "flip": np.ascontiguousarray(eye[::-1]), "bucket_of": one}


def kernel(**inputs):
    import numpy as _np
    import concourse.bacc as _bacc
    from concourse import mybir as _mybir
    from concourse.bass_utils import run_bass_kernel_spmd as _run

    nc = _bacc.Bacc("TRN2", target_bir_lowering=False, num_devices=1)
    arrays, args = {}, []
    for name, a in [(n, inputs[n]) for n in INPUTS] + list(shape_constants().items()):
        a = _np.ascontiguousarray(a)
        arrays[f"in_{name}_dram"] = a
        args.append(nc.dram_tensor(f"in_{name}_dram", a.shape, _mybir.dt.from_np(a.dtype), kind="ExternalInput").ap())
    args.append(nc.dram_tensor("out_dram", (1, SEQ, D), _mybir.dt.float32, kind="ExternalOutput").ap())
    trunk(nc, *args)
    r = _run(nc, [arrays], core_ids=[0])
    return r.results[0]["out_dram"]
```

```python
import concourse.bass as bass
from concourse import mybir
from contextlib import ExitStack

P = 128
SEQ, D, MEM = 512, 1024, 256
KD = D // P
TT = SEQ // P
MT = MEM // P
HD, NH, NKV, MH, MHD = 64, 8, 2, 4, 128
GQA = NH // NKV
CONV_W, FF = 512, 2816
CB = CONV_W // P
FB = FF // P
CHUNK = 64
WIN = 3 * CHUNK
ATT0 = 3 * CONV_W
KV0 = ATT0 + NH * HD
MQ0 = KV0 + 2 * NKV * HD
GATE0 = MQ0 + MH * MHD
EPS = 1e-6
MASKED = -1e30
REL = P + WIN

N_MEMK, N_MEMV, N_Q, N_KVM, N_MQ2, N_CONV = 0, 4, 8, 12, 16, 18
N_J, J_WT, J_IT = 30, 9, KD // 2
N_WO = N_J + J_WT * J_IT
N_UP, UP_IT = N_WO + 8, FB // 2
N_DN, DN_IT = N_UP + 4 * UP_IT, (FB // 2 - 3) // 2
N_END = N_DN + FB


def slot_of(n):
    return n % 3 if n < N_WO else (n - N_WO) % 4


def uses(n):
    return sum(slot_of(m) == slot_of(n) for m in range(n + 1))


def previous(n):
    before = [m for m in range(n) if slot_of(m) == slot_of(n)]
    return before[-1] if before else None


PROBS_AT, ATTEND = (19, 22, 25, 28), (20, 23, 26, 29)
MEM_SCORES, MEM_PROBS_AT, MEM_ATTEND = (19, 21, 24, 27), (21, 23, 26, 29), (22, 24, 27, 29)


def straight_results():
    out, free = [], [4, 5, 6, 7]

    def side(*name):
        out.append((name, free[0]))
        free.append(free.pop(0))

    def scores(t):
        for g in range(NKV):
            for r in range(2):
                side("score", t, g, r)

    def probs(t):
        for kt in ((0, 1) if t else (1,)):
            for g in range(NKV):
                side("probT", t, kt, g)

    def mem_scores(t):
        side("mscore", t, 0)
        side("mscore", t, 1)

    def mem_probs(t):
        side("mprobT", t, 0)
        side("mprobT", t, 1)

    side("gainT")
    for t in range(MT):
        side("memT", t, 0)
        side("memT", t, 1)
    for n in range(N_MEMK, N_MEMV):
        if n == N_MEMV - 1:
            out.append((("mk", 0), 0))
            out.append((("mk", 1), 1))
        else:
            out.append((("wt", n), None))
    for n in range(N_MEMV, N_Q):
        if n == N_Q - 1:
            out.append((("mv", 0), 2))
            out.append((("mv", 1), 3))
        else:
            out.append((("wt", n), None))
        if n == 4:
            side("params")
            side("relvec")
        side("xT", n - N_MEMV, 0)
        side("xT", n - N_MEMV, 1)
    for first, last, name in ((N_Q, N_KVM, "q"), (N_KVM, N_MQ2, "kvm"), (N_MQ2, N_CONV, "mq2")):
        for n in range(first, last):
            if n == last - 1:
                for t in range(TT):
                    out.append(((name, t), t))
            else:
                out.append((("wt", n), None))
            if n == 10:
                side("mkT", 0)
                side("mkT", 1)
            if n in (13, 14):
                side("qT", 2 * (n - 13))
                side("qT", 2 * (n - 13) + 1)
            if n in (16, 17):
                side("kmT", 2 * (n - 16))
                side("kmT", 2 * (n - 16) + 1)
            if n == 17:
                scores(0)
    free.insert(0, 3)
    for n in range(N_CONV, N_J):
        out.append((("conv", n), (n - N_CONV) % 3))
        if n == 18:
            side("mq2T", 0)
            side("mq2T", 1)
        if n in PROBS_AT:
            probs(PROBS_AT.index(n))
        if n in MEM_PROBS_AT:
            mem_probs(MEM_PROBS_AT.index(n))
        if n in ATTEND:
            side("attn", ATTEND.index(n))
            if n != ATTEND[-1]:
                scores(ATTEND.index(n) + 1)
        if n in MEM_ATTEND:
            side("mattn", MEM_ATTEND.index(n))
        if n in MEM_SCORES:
            mem_scores(MEM_SCORES.index(n))
    return out


RESULTS = straight_results()
BANK = {name: bank for name, bank in RESULTS}
DONE = {name: i + 1 for i, (name, _) in enumerate(RESULTS)}
NTH = {name: sum(b == bank for _, b in RESULTS[:i + 1]) for i, (name, bank) in enumerate(RESULTS)}
TAKEN0 = [sum(b == bank for _, b in RESULTS) for bank in range(8)]
DONE0 = len(RESULTS)
J_DONE, UP_DONE, DN_DONE = 12, 4, 4
DONE_WO = DONE0 + J_DONE * J_IT
J_TAKEN = [2, 2, 2, 2, 1, 1, 1, 1]
TAKEN_WO = [a + J_IT * b for a, b in zip(TAKEN0, J_TAKEN)]
WO_ORDER = [("wo", 0), ("wo", 1), ("h2T", 0), ("wo", 2), ("h2T", 1), ("w", 70), ("w", 71), ("w", 72), ("wo", 3),
            ("h2T", 2), ("h2T", 3)]
WO_AT, _at = {}, DONE_WO + 7
for _name in WO_ORDER:
    _at += 2 if _name[0] == "h2T" else 1
    WO_AT[_name] = _at
DONE_UP = _at
TAKEN_UP = [TAKEN_WO[b] + (3 if b < 4 else 1) for b in range(8)]
DONE_DN = DONE_UP + UP_DONE * UP_IT
TAKEN_DN = [TAKEN_UP[b] + (UP_IT if b >= 4 else 0) for b in range(8)]


def last_name(n):
    if n == N_MEMV - 1:
        return ("mk", 1)
    if n == N_Q - 1:
        return ("mv", 1)
    for last, name in ((N_KVM, "q"), (N_MQ2, "kvm"), (N_CONV, "mq2")):
        if n == last - 1:
            return (name, TT - 1)
    return ("conv", n) if n >= N_CONV else ("wt", n)


NORMED_MK = TT
NORMED_Q = NORMED_MK + MT
NORMED_KM, NORMED_MQ2, NORMED_H2 = NORMED_Q + TT, NORMED_Q + 2 * TT, NORMED_Q + 3 * TT
PARAM_DMAS = 9
ROW_SUMS = ((MT,), (MT + 1,), (MT + 2,), (MT + 3,), (0,), (1,))
ROOT_NTH = {c: i + 1 for i, c in enumerate(sum(ROW_SUMS, ()))}
J_USED = [1, 2, 3, 4, 5, 6, 8, 10, 12]


def used(n):
    if n < N_J:
        return DONE[last_name(n)]
    if n < N_WO:
        return DONE0 + (n - N_J) // J_WT * J_DONE + J_USED[(n - N_J) % J_WT]
    if n < N_WO + 3:
        return DONE_WO + n - N_WO + 1
    if n == N_WO + 3:
        return DONE_WO + 7
    if n < N_UP:
        return WO_AT[("w", n)] if n < N_UP - 1 else WO_AT[("wo", 3)]
    return DONE_UP + n - N_UP + 1


def line(value, n, i, period):
    step = value(n + 2 * period) - value(n + period)
    assert value(n + period) - step >= value(n)
    return value(n + period) - step + i * step


def trunk(nc, x, mem, rel_bias, norm_mix, norm_mem, norm_ffn, w_in, b_gate, conv_w, q_norm, k_norm, sinks,
          mq_norm, mk_norm, w_mem_kv, w_br_conv, w_br_attn, w_br_mem, w_o, w_up, ffn_conv_w, ffn_conv_b, w_down,
          eye, bucket_of, out):
    f32, f32r = mybir.dt.float32, mybir.dt.float32r
    ALU, ACT, AX = mybir.AluOpType, mybir.ActivationFunctionType, mybir.AxisListType
    ds = bass.ds

    win_v = w_in[0].rearrange("(k p) c -> p k c", p=P)
    wkv_v = w_mem_kv[0].rearrange("(k p) c -> p k c", p=P)
    wbr_v = [w[0].rearrange("(k p) c -> p k c", p=P) for w in (w_br_conv, w_br_attn, w_br_mem)]
    wo_v = w_o[0].rearrange("(k p) c -> p k c", p=P)
    wup_v = w_up[0].rearrange("(k p) c -> p k c", p=P)
    wdn_v = w_down[0].rearrange("(k p) c -> p k c", p=P)
    x_v = x[0].rearrange("(t p) d -> p t d", p=P)
    mem_v = mem[0].rearrange("(t p) d -> p t d", p=P)
    out_v = out[0].rearrange("(t p) d -> p t d", p=P)
    rel_dram = nc.dram_tensor("rel_dram", (NH, REL), f32, kind="Internal").ap()

    ctx = ExitStack()
    with ctx:
        def sb(name, shape, dt):
            return ctx.enter_context(nc.sbuf_tensor(name, shape, dt))

        def sem(name):
            return ctx.enter_context(nc.semaphore(name))

        stage = sb("stage", [P, 4, 1024], f32)
        w_hi = sb("w_hi", [P, 4, 1024], f32r)
        w_lo = sb("w_lo", [P, 4, 1024], f32r)
        h_hi = sb("h_hi", [P, KD, SEQ], f32r)
        h_lo = sb("h_lo", [P, KD, SEQ], f32r)
        a_hi = sb("a_hi", [P, 12, SEQ], f32r)
        a_lo = sb("a_lo", [P, 12, SEQ], f32r)
        arena = sb("arena", [P, 16384], f32)
        temp = sb("temp", [P, 4, SEQ], f32)
        ident = sb("ident", [P, P], f32)
        cols = sb("cols", [P, 224], f32)
        stat = sb("stat", [P, 120], f32)

        x_t = arena[:, 0:4096].rearrange("p (t d) -> p t d", t=TT)
        qT = arena[:, 0:2048].rearrange("p (b s) -> p b s", b=4)
        mqT = arena[:, 2048:4096].rearrange("p (b s) -> p b s", b=4)
        raw_a = arena[:, 4096:6144].rearrange("p (t c) -> p t c", t=TT)
        probs = arena[:, 6144:8192].rearrange("p (h c) -> p h c", h=NH)
        raw_b = arena[:, 6144:8192].rearrange("p (t c) -> p t c", t=TT)
        mem_t = arena[:, 6144:8192].rearrange("p (t d) -> p t d", t=MT)
        rel_flip = arena[:, 6144:6144 + NH * WIN].rearrange("p (h c) -> p h c", h=NH)
        probT = arena[:, 4096:6144].rearrange("p (k g r c) -> p k g r c", k=2, g=NKV, r=2)
        kT = arena[:, 8192:9216].rearrange("p (g s) -> p g s", g=NKV)
        params = arena[:, 8192:8192 + 3 * P].rearrange("p (a c) -> p a c", a=3)
        mkT = arena[:, 9216:10240].rearrange("p (h s) -> p h s", h=MH)
        m_v = arena[:, 10240:11264].rearrange("p (t c) -> p t c", t=MT)
        v_t = arena[:, 11264:11776].rearrange("p (t c) -> p t c", t=TT)
        bias = arena[:, 11776:11776 + NH * WIN].rearrange("p (h c) -> p h c", h=NH)
        mprobs = arena[:, 13312:14336].rearrange("p (h c) -> p h c", h=MH)
        mprobT = arena[:, 14336:15360].rearrange("p (k c) -> p k c", k=2)
        gain_rows = arena[0:KD, 13312:13312 + P]
        gain_mix = arena[:, 14336:15360]
        mk_raw = arena[:, 15360:16384].rearrange("p (t c) -> p t c", t=MT)
        sig = arena[:, 0:3072].rearrange("p (b s) -> p b s", b=6)
        merged = arena[:, 4096:8192]
        merge_tmp = arena[:, 8192:9216].rearrange("p (b s) -> p b s", b=2)
        act = arena[:, 0:FB * SEQ]
        gain_ffn = arena[:, 11264:12288]
        x2 = arena[:, 12288:16384].rearrange("p (t d) -> p t d", t=TT)
        temp2 = temp[:, :, :].rearrange("p (a b) s -> p a (b s)", b=2)
        onehot = temp[0:32, 2, 0:REL]
        rel_sb = temp[0:32, 3, 0:NH]
        rel_row = temp[0:NH, 3, NH:NH + REL]

        memT_hi = a_hi[:, 0:4, :].rearrange("p a b -> p (a b)").rearrange("p (k s) -> p k s", k=KD)
        memT_lo = a_lo[:, 0:4, :].rearrange("p a b -> p (a b)").rearrange("p (k s) -> p k s", k=KD)
        aring_hi = h_hi[:, 0:4, :].rearrange("p a b -> p (a b)")
        aring_lo = h_lo[:, 0:4, :].rearrange("p a b -> p (a b)")

        bg_col = cols[:, 0:24]
        cw_col = cols[:, 24:36]
        qg, kg, mqg, mkg = (cols[:, c:c + 1] for c in (36, 37, 38, 39))
        fb_col = cols[:, 40:40 + FB * 2]
        fw_col = cols[:, 84:84 + 3 * 2 * FB]
        mem_gain = cols[:, 216:216 + KD]
        neg_half = stat[:, 0:8]
        sink = stat[:, 8:16]
        ss = stat[:, 16:24]
        hv = stat[:, 32:64].rearrange("p (t c) -> p t c", t=TT)
        kv_ = stat[:, 64:80].rearrange("p (t c) -> p t c", t=TT)
        mk_ = stat[:, 64:72].rearrange("p (t c) -> p t c", t=MT)
        mq_ = stat[:, 80:88].rearrange("p (t c) -> p t c", t=TT)
        top, den = stat[:, 88:96], stat[:, 96:104]
        mtop, mden = stat[:, 104:108], stat[:, 108:112]
        unread = stat[:, 112:120]
        sink_e = stat[:, 32:40]
        ss2a, ss2b = stat[:, 16:20], stat[:, 20:24]

        bank = [ctx.enter_context(nc.psum_tensor(f"bank{b}", [P, 512], f32)) for b in range(8)]

        w_loaded = [sem(f"w_loaded{s}") for s in range(4)]
        hi_ready = sem("hi_ready")
        lo_ready = sem("lo_ready")
        pe_done = sem("pe_done")
        taken = [sem(f"taken{b}") for b in range(8)]
        mem_in = [sem(f"mem_in{t}") for t in range(MT)]
        x_in = [sem(f"x_in{t}") for t in range(TT)]
        gain_mem_in = sem("gain_mem_in")
        gain_mix_in = sem("gain_mix_in")
        eye_in = sem("eye_in")
        params_in = sem("params_in")
        rel_in = sem("rel_in")
        sink_in = sem("sink_in")
        relvec_out = sem("relvec_out")
        relflip_in = sem("relflip_in")
        x_again = sem("x_again")
        ffn_gain_in = sem("ffn_gain_in")
        stored = sem("stored")
        squares = sem("squares")
        var_ready = sem("var_ready")
        pow_ready = sem("pow_ready")
        normed = sem("normed")
        hi_taken = sem("hi_taken")
        sq_ready = sem("sq_ready")
        v_ready = sem("v_ready")
        params_done = sem("params_done")
        maxed = sem("maxed")
        expd = sem("expd")
        recip = sem("recip")
        probs_ready = sem("probs_ready")
        mmaxed = sem("mmaxed")
        mrecip = sem("mrecip")
        mprobs_ready = sem("mprobs_ready")
        zeroed = sem("zeroed")
        conv_hi = sem("conv_hi")
        conv_x = sem("conv_x")
        conv_lo = sem("conv_lo")
        merged_ready = sem("merged_ready")
        merged_hi = sem("merged_hi")
        merged_lo = sem("merged_lo")
        tap_ready = sem("tap_ready")
        silu_ready = sem("silu_ready")
        act_ready = sem("act_ready")
        ring_hi = sem("ring_hi")
        ring_lo = sem("ring_lo")
        final = sem("final")
        dve_chain = sem("dve_chain")

        block = ctx.enter_context(nc.Block())

        def matmul3(dst, stat_hi, stat_lo, mov_hi, mov_lo, first, last):
            nc.tensor.matmul(dst, stat_hi, mov_hi, start=first, stop=False)
            nc.tensor.matmul(dst, stat_hi, mov_lo, start=False, stop=False)
            return nc.tensor.matmul(dst, stat_lo, mov_hi, start=False, stop=last)

        def wait_taken(engine, name):
            engine.wait_ge(taken[BANK[name]], NTH[name])

        def mem_gain_of(n, k):
            kb = n % 4 * 2 + k
            return mem_gain[:, kb:kb + 1]

        @block.tensor
        def _(pe):
            at = [0]

            def finished(name, ins):
                assert RESULTS[at[0]][0] == name, (RESULTS[at[0]], name)
                at[0] += 1
                ins.then_inc(pe_done, 1)

            def bank_for(name):
                b = BANK[name]
                if NTH[name] > 1:
                    pe.wait_ge(taken[b], NTH[name] - 1)
                return bank[b]

            def was_taken(name):
                wait_taken(pe, name)

            def transposes(name, sources, at_bank=None):
                ps = bank_for(name)
                for c, src in enumerate(sources):
                    last = nc.tensor.transpose(ps[:, c * P:(c + 1) * P], src, ident[:, :])
                finished(name, last)

            def tokens_stationary(n, first, last_n, names, lhs, width, count, tile=None):
                kk = 1024 // width
                pe.wait_ge(lo_ready, n + 1)
                s = slot_of(n)
                for t in range(count):
                    if n == first:
                        bank_for(names[t])
                    if tile is not None:
                        tile(t)
                    for k in range(kk):
                        kb = (n - first) * kk + k
                        last = matmul3(bank[BANK[names[t]]][:, 0:width],
                                       lhs[0][:, kb, t * P:(t + 1) * P], lhs[1][:, kb, t * P:(t + 1) * P],
                                       w_hi[:, s, k * width:(k + 1) * width], w_lo[:, s, k * width:(k + 1) * width],
                                       kb == 0, kb == KD - 1)
                    if n == last_n:
                        finished(names[t], last)
                if n != last_n:
                    finished(("wt", n), last)

            def feature_block(ps, s, rhs, blocks=KD, width=P, c=0, start=0):
                for k in range(blocks):
                    a = k * width + c * P
                    last = matmul3(ps[:, :], w_hi[:, s, a:a + P], w_lo[:, s, a:a + P],
                                   rhs[0][:, start + k, :], rhs[1][:, start + k, :], k == 0, k == blocks - 1)
                return last

            pe.wait_ge(eye_in, 16)
            pe.wait_ge(gain_mem_in, 16)
            finished(("gainT",), nc.tensor.transpose(bank_for(("gainT",))[:, 0:KD], gain_rows, ident[0:KD, 0:KD]))
            for t in range(MT):
                pe.wait_ge(mem_in[t], 16)
                for half in range(2):
                    transposes(("memT", t, half), [mem_t[:, t, (4 * half + c) * P:(4 * half + c + 1) * P]
                                                   for c in range(4)])
            def x_transposes(t):
                pe.wait_ge(normed, t + 1)
                for half in range(2):
                    transposes(("xT", t, half), [x_t[:, t, (4 * half + c) * P:(4 * half + c + 1) * P]
                                                 for c in range(4)])

            for n in range(N_MEMK, N_Q):
                first, name = (N_MEMK, "mk") if n < N_MEMV else (N_MEMV, "mv")
                tokens_stationary(n, first, first + 3, [(name, t) for t in range(MT)], (memT_hi, memT_lo), 512, MT,
                                  (lambda t: was_taken(("memT", t, n // 2))) if n in (0, 2) else None)
                if n == 4:
                    pe.wait_ge(params_in, PARAM_DMAS * 16)
                    ps = bank_for(("params",))
                    nc.tensor.transpose(ps[:, 0:84], params[0:84, 0, :], ident[0:84, 0:84])
                    nc.tensor.transpose(ps[:, 84:172], params[0:88, 1, :], ident[0:88, 0:88])
                    finished(("params",), nc.tensor.transpose(ps[:, 172:216], params[0:44, 2, :], ident[0:44, 0:44]))
                    pe.wait_ge(rel_in, 32)
                    finished(("relvec",), nc.tensor.matmul(bank_for(("relvec",))[0:NH, 0:REL], rel_sb, onehot,
                                                           start=True, stop=True))
                if n >= N_MEMV:
                    x_transposes(n - N_MEMV)
            h = (h_hi, h_lo)
            for n in range(N_Q, N_CONV):
                if n < N_KVM:
                    tokens_stationary(n, N_Q, N_KVM - 1, [("q", t) for t in range(TT)], h, 512, TT,
                                      (lambda t: was_taken(("xT", t, (n - N_Q) // 2))) if n in (N_Q, N_Q + 2) else None)
                elif n < N_MQ2:
                    tokens_stationary(n, N_KVM, N_MQ2 - 1, [("kvm", t) for t in range(TT)], h, 512, TT)
                else:
                    tokens_stationary(n, N_MQ2, N_CONV - 1, [("mq2", t) for t in range(TT)], h, 256, TT)
                if n == 10:
                    for t in range(MT):
                        pe.wait_ge(normed, NORMED_MK + t + 1)
                        transposes(("mkT", t), [mk_raw[:, t, head * P:(head + 1) * P] for head in range(MH)])
                if n in (13, 14):
                    for t in (2 * (n - 13), 2 * (n - 13) + 1):
                        pe.wait_ge(normed, NORMED_Q + t + 1)
                        transposes(("qT", t), [raw_a[:, t, c * P:(c + 1) * P] for c in range(4)])

                def key_transposes(t):
                    pe.wait_ge(normed, NORMED_KM + t + 1)
                    transposes(("kmT", t), [temp[:, t, 0:P], temp[:, t, P:2 * P],
                                            raw_b[:, t, 256:384], raw_b[:, t, 384:512]])
                if n in (16, 17):
                    key_transposes(2 * (n - 16))
                    key_transposes(2 * (n - 16) + 1)

            def scores(t):
                was_taken(("qT", t))
                was_taken(("kmT", t))
                lo = 0 if t else CHUNK
                for g in range(NKV):
                    for r in range(2):
                        name = ("score", t, g, r)
                        ps = bank_for(name)
                        for i in range(2):
                            last = nc.tensor.matmul(
                                ps[:, i * WIN + lo:(i + 1) * WIN],
                                qT[64 * r:64 * r + 64, 2 * g + i, t * P:(t + 1) * P],
                                kT[64 * r:64 * r + 64, g, t * P - CHUNK + lo:(t + 1) * P], start=True, stop=True)
                        finished(name, last)

            def prob_transposes(t):
                pe.wait_ge(probs_ready, t + 1)
                for kt in ((0, 1) if t else (1,)):
                    for g in range(NKV):
                        transposes(("probT", t, kt, g), [probs[:, 4 * g + 2 * i + r, kt * P:(kt + 1) * P]
                                                         for r in range(2) for i in range(2)])

            def attend(t):
                kts = (0, 1) if t else (1,)
                for kt in kts:
                    for g in range(NKV):
                        was_taken(("probT", t, kt, g))
                if t == 0:
                    pe.wait_ge(v_ready, TT)
                name = ("attn", t)
                ps = bank_for(name)
                for g in range(NKV):
                    for r in range(2):
                        for kt in kts:
                            last = nc.tensor.matmul(ps[64 * r:64 * r + 64, g * 256:(g + 1) * 256],
                                                    v_t[:, t - 1 + kt, g * HD:(g + 1) * HD],
                                                    probT[:, kt, g, r, :], start=(kt == kts[0]), stop=(kt == 1))
                finished(name, last)

            def mem_scores(t):
                for a in range(2):
                    name = ("mscore", t, a)
                    if a == 0:
                        was_taken(("mkT", 0))
                        was_taken(("mkT", 1))
                        was_taken(("kmT", t))
                    else:
                        was_taken(("mq2T", t // 2))
                    ps = bank_for(name)
                    for i in range(2):
                        last = nc.tensor.matmul(ps[:, i * MEM:(i + 1) * MEM], mqT[:, 2 * a + i, t * P:(t + 1) * P],
                                                mkT[:, 2 * a + i, :], start=True, stop=True)
                    finished(name, last)

            def mem_prob_transposes(t):
                pe.wait_ge(mprobs_ready, t + 1)
                for kt in range(2):
                    transposes(("mprobT", t, kt), [mprobs[:, i, kt * P:(kt + 1) * P] for i in range(MH)])

            def mem_attend(t):
                for kt in range(2):
                    was_taken(("mprobT", t, kt))
                was_taken(("mv", 1))
                name = ("mattn", t)
                ps = bank_for(name)
                for i in range(MH):
                    for kt in range(2):
                        last = nc.tensor.matmul(ps[:, i * P:(i + 1) * P], m_v[:, kt, i * P:(i + 1) * P],
                                                mprobT[:, kt, i * P:(i + 1) * P], start=(kt == 0), stop=(kt == 1))
                finished(name, last)

            scores(0)
            for n in range(N_CONV, N_J):
                name = ("conv", n)
                ps = bank_for(name)
                pe.wait_ge(lo_ready, n + 1)
                finished(name, feature_block(ps, slot_of(n), h))
                if n == 18:
                    for a in range(2):
                        pe.wait_ge(normed, NORMED_MQ2 + 2 * a + 2)
                        transposes(("mq2T", a), [raw_a[:, 2 * a + tt, c * P:(c + 1) * P]
                                                 for tt in range(2) for c in range(2)])
                if n in PROBS_AT:
                    prob_transposes(PROBS_AT.index(n))
                if n in MEM_PROBS_AT:
                    mem_prob_transposes(MEM_PROBS_AT.index(n))
                if n in ATTEND:
                    attend(ATTEND.index(n))
                    if n != ATTEND[-1]:
                        scores(ATTEND.index(n) + 1)
                if n in MEM_ATTEND:
                    mem_attend(MEM_ATTEND.index(n))
                if n in MEM_SCORES:
                    mem_scores(MEM_SCORES.index(n))
            assert at[0] == len(RESULTS)

            a_in = (a_hi, a_lo)
            def merge_pair(i):
                for r in range(J_WT):
                    n = N_J + r
                    pe.wait_ge(lo_ready, i * J_WT + n + 1)
                    if r < 6:
                        b = r % 4
                        pe.wait_ge(taken[b], i * J_TAKEN[b] + TAKEN0[b] + (r >= 4))
                        feature_block(bank[b], slot_of(n), h).then_inc(pe_done, 1)
                        continue
                    if r == 6:
                        pe.wait_ge(conv_lo, CB)
                    if r == 7:
                        for b in range(4, 8):
                            pe.wait_ge(taken[b], TAKEN0[b])
                    for jj in range(2):
                        b = 2 + 2 * (r - 6) + jj
                        pe.wait_ge(taken[b], i * J_TAKEN[b] + TAKEN0[b] + (b < 4))
                        feature_block(bank[b], slot_of(n), a_in, blocks=4, width=256, c=jj,
                                      start=4 * (r - 6)).then_inc(pe_done, 1)

            with pe.Fori(0, J_IT - 1) as i:
                merge_pair(i)
            merge_pair(J_IT - 1)

            def wo_part(n, t, b):
                kb = (n - N_WO) % 4 * 2
                for k in range(2):
                    tokens, columns = slice(t * P, (t + 1) * P), slice(k * 512, (k + 1) * 512)
                    last = matmul3(bank[b][:, :], h_hi[:, kb + k, tokens], h_lo[:, kb + k, tokens],
                                   w_hi[:, slot_of(n), columns], w_lo[:, slot_of(n), columns],
                                   kb + k == 0, kb + k == KD - 1)
                return last

            for n in range(N_WO, N_WO + 4):
                pe.wait_ge(lo_ready, n + 1)
                pe.wait_ge(merged_lo, 2 * (n - N_WO) + 2)
                for t in range(TT):
                    if n == N_WO:
                        pe.wait_ge(taken[t], TAKEN_WO[t])
                    last = wo_part(n, t, t)
                    if n == N_WO + 3:
                        last.then_inc(pe_done, 1)
                if n < N_WO + 3:
                    last.then_inc(pe_done, 1)
            for t in range(TT):
                pe.wait_ge(taken[4 + t], TAKEN_WO[4 + t])
                for n in range(N_WO + 4, N_UP):
                    if t == 0:
                        pe.wait_ge(lo_ready, n + 1)
                    last = wo_part(n, t, 4 + t)
                    if t == TT - 1 or n == N_UP - 1:
                        last.then_inc(pe_done, 1)

                def h2_transposes(t):
                    pe.wait_ge(normed, NORMED_H2 + t + 1)
                    for half in range(2):
                        b = 2 * (t % 2) + half
                        pe.wait_ge(taken[b], TAKEN_WO[b] + 1 + t // 2)
                        for c in range(4):
                            last = nc.tensor.transpose(bank[b][:, c * P:(c + 1) * P],
                                                       temp2[:, t % 2, (4 * half + c) * P:(4 * half + c + 1) * P],
                                                       ident[:, :])
                        last.then_inc(pe_done, 1)
                if t:
                    h2_transposes(t - 1)

            def up_part(r, half, blocks=range(KD)):
                at = slice(half * 256, (half + 1) * 256)
                for k in blocks:
                    last = matmul3(bank[4 + r][:, at], w_hi[:, r, k * P:(k + 1) * P], w_lo[:, r, k * P:(k + 1) * P],
                                   a_hi[:, k, at], a_lo[:, k, at], k == 0, k == KD - 1)
                return last

            for b in range(4):
                pe.wait_ge(taken[b], TAKEN_WO[b] + 2)
            for r in range(2):
                pe.wait_ge(lo_ready, N_UP + r + 1)
                pe.wait_ge(taken[4 + r], TAKEN_UP[4 + r])
                if r == 0:
                    up_part(r, 0)
            up_part(1, 0, range(5))
            h2_transposes(TT - 1)
            up_part(1, 0, range(5, KD))
            for r in range(2):
                for half in range(2):
                    pe.wait_ge(taken[half], TAKEN_UP[half])
                    pe.wait_ge(taken[2 + half], TAKEN_UP[2 + half])
                    last = up_part(r, 1, range(4 * half, 4 * half + 4))
                last.then_inc(pe_done, 1)
            for r in range(2, 4):
                pe.wait_ge(lo_ready, N_UP + r + 1)
                pe.wait_ge(taken[4 + r], TAKEN_UP[4 + r])
                feature_block(bank[4 + r], slot_of(N_UP + r), a_in).then_inc(pe_done, 1)

            def up_pair(i):
                for r in range(4):
                    n = N_UP + r
                    pe.wait_ge(lo_ready, i * 4 + n + 1)
                    pe.wait_ge(taken[4 + r], i + TAKEN_UP[4 + r])
                    feature_block(bank[4 + r], slot_of(n), a_in).then_inc(pe_done, 1)

            with pe.Fori(1, UP_IT - 1) as i:
                up_pair(i)
            up_pair(UP_IT - 1)

            def down_part(m, half, t, s, first, last_block):
                for k in range(2):
                    a = (m % 2 * 2 + k) * SEQ + t * P
                    last = matmul3(bank[4 * half + t][:, :], aring_hi[:, a:a + P], aring_lo[:, a:a + P],
                                   w_hi[:, s, k * 512:(k + 1) * 512], w_lo[:, s, k * 512:(k + 1) * 512],
                                   first and k == 0, last_block and k == 1)
                return last

            def down_pair(m, i, first):
                pe.wait_ge(ring_lo, i * 2 + m + 1)
                for half in range(2):
                    n = N_DN + 2 * m + half
                    pe.wait_ge(lo_ready, i * 4 + n + 1)
                    for t in range(TT):
                        if first:
                            pe.wait_ge(taken[4 * half + t], TAKEN_DN[4 * half + t])
                        last = down_part(m, half, t, slot_of(n), first, False)
                    last.then_inc(pe_done, 1)

            down_pair(0, 0, True)
            with pe.Fori(0, DN_IT) as i:
                down_pair(1, i, False)
                down_pair(2, i, False)
            down_pair(FB // 2 - 2, 0, False)
            pe.wait_ge(ring_lo, FB // 2)
            pe.wait_ge(lo_ready, N_END)
            for t in range(TT):
                for half in range(2):
                    down_part(FB // 2 - 1, half, t, slot_of(N_END - 2 + half), False, True).then_inc(pe_done, 1)

        @block.sync
        def _(sp):
            def load(n, src, width, i=0, period=0):
                if n == N_J + 5:
                    sp.wait_ge(lo_ready, i * period + previous(n + 1) + 1)
                elif period and n != N_J + 6:
                    sp.wait_ge(lo_ready, i * period + previous(n) + 1)
                elif not period and previous(n) is not None:
                    sp.wait_ge(lo_ready, previous(n) + 1)
                s = slot_of(n)
                sp.dma_start(stage[:, s, :].rearrange("p (k c) -> p k c", c=width), src).then_inc(w_loaded[s], 16)

            sp.dma_start(ident[:, :], eye).then_inc(eye_in, 16)
            for n in range(N_MEMK, N_Q):
                r = n % 4
                load(n, wkv_v[:, 2 * r:2 * r + 2, (n // 4) * 512:(n // 4 + 1) * 512], 512)
                if n == 0:
                    sp.dma_start(mem_t[:, 1, :], mem_v[:, 1, :]).then_inc(mem_in[1], 16)
                if 2 <= n < 2 + TT:
                    sp.dma_start(x_t[:, n - 2, :], x_v[:, n - 2, :]).then_inc(x_in[n - 2], 16)
                if n == 3:
                    sp.dma_start(gain_mix, norm_mix.broadcast_to([P, D])).then_inc(gain_mix_in, 16)
                if n == 5:
                    sp.dma_start(rel_sb, rel_bias).then_inc(rel_in, 16)
                    sp.dma_start(onehot, bucket_of).then_inc(rel_in, 16)
                    for dst, src in (
                        (params[0:24, 0, :], b_gate[0].rearrange("(b c) -> b c", c=P)),
                        (params[24:36, 0, :], conv_w[0].rearrange("a (b c) -> (a b) c", c=P)),
                        (params[36:37, 0, :].rearrange("p (a c) -> p a c", a=2),
                         q_norm.unsqueeze(1).broadcast_to([1, 2, HD])),
                        (params[37:38, 0, :].rearrange("p (a c) -> p a c", a=2),
                         k_norm.unsqueeze(1).broadcast_to([1, 2, HD])),
                        (params[38:39, 0, :], mq_norm),
                        (params[39:40, 0, :], mk_norm),
                        (params[40:84, 0, :], ffn_conv_b[0].rearrange("(b c) -> b c", c=P)),
                        (params[0:88, 1, :], ffn_conv_w[0, 0:2, :].rearrange("a (b c) -> (a b) c", c=P)),
                        (params[0:44, 2, :], ffn_conv_w[0, 2, :].rearrange("(b c) -> b c", c=P)),
                    ):
                        sp.dma_start(dst, src).then_inc(params_in, 16)
                    sp.dma_start(sink, sinks.broadcast_to([P, NH])).then_inc(sink_in, 16)
            for n in range(N_Q, N_CONV):
                if n < N_MQ2:
                    r, c0 = n % 4, ATT0 + (n - N_Q) // 4 * 512
                    load(n, win_v[:, 2 * r:2 * r + 2, c0:c0 + 512], 512)
                else:
                    r, c0 = n - N_MQ2, MQ0 + 256
                    load(n, win_v[:, 4 * r:4 * r + 4, c0:c0 + 256], 256)
            for n in range(N_CONV, N_J):
                r = n - N_CONV
                c0 = (CONV_W, 2 * CONV_W, 0)[r % 6 // 2] + (r // 6 * 2 + r % 2) * P
                load(n, win_v[:, :, c0:c0 + P], P)
            with sp.Fori(0, J_IT) as i:
                for r in range(J_WT):
                    if r < 6:
                        load(N_J + r, win_v[:, :, ds(i * 256 + (GATE0 + r // 2 * D + r % 2 * P), P)], P, i, J_WT)
                    else:
                        load(N_J + r, wbr_v[r - 6][:, :, ds(i * 256, 256)], 256, i, J_WT)
            sp.wait_ge(pe_done, DONE0 + J_DONE)
            sp.dma_start(x2, x_v).then_inc(x_again, 16)
            sp.dma_start(gain_ffn, norm_ffn.broadcast_to([P, D])).then_inc(ffn_gain_in, 16)
            for n in range(N_WO, N_UP):
                r = n - N_WO
                load(n, wo_v[:, r % 4 * 2:r % 4 * 2 + 2, r // 4 * 512:(r // 4 + 1) * 512], 512)
            with sp.Fori(0, UP_IT) as i:
                for r in range(4):
                    load(N_UP + r, wup_v[:, :, ds(i * 256 + (r % 2 * FF + r // 2 * P), P)], P, i, 4)
            with sp.Fori(0, FB // 4) as i:
                for r in range(4):
                    load(N_DN + r, wdn_v[:, ds(i * 4 + r // 2 * 2, 2), r % 2 * 512:(r % 2 + 1) * 512], 512, i, 4)
            for half in range(2):
                load(N_END - 2 + half, wdn_v[:, FB - 2:FB, half * 512:(half + 1) * 512], 512)
            for t in range(TT - 1):
                sp.wait_ge(final, 2 * t + 2)
                sp.dma_start(out_v[:, t, :], x2[:, t, :]).then_inc(stored, 16)
            for half in range(2):
                sp.wait_ge(final, 2 * TT - 1 + half)
                sp.dma_start(out_v[:, TT - 1, half * 512:(half + 1) * 512], x2[:, TT - 1, half * 512:(half + 1) * 512])\
                    .then_inc(stored, 16)
            sp.wait_ge(stored, 16 * (TT + 1))

        @block.gpsimd
        def _(pool):
            count = [0]

            def inverse_root(v, width):
                count[0] += 1
                pool.wait_ge(var_ready, count[0])
                nc.gpsimd.tensor_tensor(v, v, neg_half[:, 0:width], ALU.pow).then_inc(pow_ready, 1)

            nc.gpsimd.memset(neg_half, -0.5).then_inc(zeroed, 1)
            pool.wait_ge(zeroed, 1)
            for c in ROOT_NTH:
                inverse_root(ss[:, c:c + 1], 1)
            wait_taken(pool, ("relvec",))
            pool.dma_start(rel_dram, rel_row).then_inc(relvec_out, 16)
            pool.wait_ge(relvec_out, 16)
            pool.wait_ge(pe_done, DONE[("memT", 1, 1)])
            pool.dma_start(rel_flip, bass.AP(tensor=rel_dram.tensor, offset=0,
                                             ap=[[1, P], [REL, NH], [1, WIN]])).then_inc(relflip_in, 16)
            for t in range(MT):
                wait_taken(pool, ("mk", t))
                nc.gpsimd.tensor_tensor(temp[:, t, :], mk_raw[:, t, :], mk_raw[:, t, :], ALU.mult).then_inc(sq_ready, 1)
            for t in range(MT):
                inverse_root(mk_[:, t, :], MH)
            for t in range(TT):
                wait_taken(pool, ("q", t))
                if t == 0:
                    pool.wait_ge(relflip_in, 16)
                nc.gpsimd.tensor_tensor(temp[:, t, :], raw_a[:, t, :], raw_a[:, t, :], ALU.mult).then_inc(sq_ready, 1)
            for t in range(TT):
                inverse_root(hv[:, t, :], NH)
            for pair in ((0, 1), (2, 3)):
                for t in pair:
                    wait_taken(pool, ("kvm", t))
                    nc.gpsimd.tensor_tensor(temp[:, t, :], raw_b[:, t, :], raw_b[:, t, :], ALU.mult)\
                        .then_inc(sq_ready, 1)
                for t in pair:
                    inverse_root(kv_[:, t, :], 4)
            for t in range(TT):
                nc.gpsimd.tensor_copy(v_t[:, t, :], raw_b[:, t, P:2 * P]).then_inc(v_ready, 1)
            for t in range(TT):
                wait_taken(pool, ("mq2", t))
                nc.gpsimd.tensor_tensor(temp[:, t, 256:512], raw_a[:, t, 0:256], raw_a[:, t, 0:256],
                                        ALU.mult).then_inc(sq_ready, 1)
            for t in range(TT):
                inverse_root(mq_[:, t, 0:2], 2)
            pool.wait_ge(pe_done, DONE[("kmT", TT - 1)])
            nc.gpsimd.memset(probs[:, :, 0:CHUNK], 0.0).then_inc(zeroed, 1)
            pool.wait_ge(zeroed, 2)

            def normalise(t):
                lo = 0 if t else CHUNK
                pool.wait_ge(recip, t + 1)
                p = probs[:, :, CHUNK + lo:256]
                nc.gpsimd.tensor_tensor(p, p, den[:, :].unsqueeze(2).broadcast_to([P, NH, WIN - lo]),
                                        ALU.mult).then_inc(probs_ready, 1)

            def mem_normalise(t):
                pool.wait_ge(mrecip, t + 1)
                nc.gpsimd.tensor_tensor(mprobs, mprobs, mden[:, :].unsqueeze(2).broadcast_to([P, MH, MEM]),
                                        ALU.mult).then_inc(mprobs_ready, 1)

            for t in range(TT):
                normalise(t)
                mem_normalise(t)
            for t in range(TT):
                inverse_root(ss[:, t:t + 1], 1)

        @block.scalar
        def _(act_):
            def split_hi(n, i=0, period=0):
                s = slot_of(n)
                if period:
                    act_.wait_ge(w_loaded[s], line(lambda m: 16 * uses(m), n, i, period))
                    act_.wait_ge(pe_done, line(lambda m: used(previous(m)), n, i, period))
                else:
                    act_.wait_ge(w_loaded[s], 16 * uses(n))
                    if previous(n) is not None:
                        act_.wait_ge(pe_done, used(previous(n)))
                if n < N_Q:
                    for k in range(2):
                        at = slice(k * 512, (k + 1) * 512)
                        ins = nc.scalar.activation(w_hi[:, s, at], stage[:, s, at], ACT.Copy, scale=mem_gain_of(n, k))
                    ins.then_inc(hi_ready, 1)
                    return
                nc.scalar.activation(w_hi[:, s, :], stage[:, s, :], ACT.Copy).then_inc(hi_ready, 1)

            def take(name, dst, scale=None, columns=slice(0, 512), frees=True):
                act_.wait_ge(pe_done, DONE[name])
                src = bank[BANK[name]][:, columns]
                if len(dst.shape) == 3:
                    src = src.rearrange("p (a c) -> p a c", a=dst.shape[1])
                if len(dst.shape) == 4:
                    src = src.rearrange("p (a b c) -> p a b c", a=dst.shape[1], b=dst.shape[2])
                ins = nc.scalar.activation(dst, src, ACT.Copy, scale=1.0 if scale is None else scale)
                ins.then_inc(taken[BANK[name]] if frees else hi_taken, 1)

            act_.dma_start(gain_rows, norm_mem[0].rearrange("(k c) -> k c", c=P)).then_inc(gain_mem_in, 16)
            act_.dma_start(mem_t[:, 0, :], mem_v[:, 0, :]).then_inc(mem_in[0], 16)

            squared = [0]

            def square(src, junk, total):
                if squared[0]:
                    act_.wait_ge(squares, squared[0])
                squared[0] += 1
                nc.scalar.activation(junk, src, ACT.Square, accum_out=total).then_inc(squares, 1)

            junk = arena[:, 4096:5120]
            act_.wait_ge(zeroed, 1)
            nc.scalar.activation(unread, neg_half, ACT.Copy)
            wait_taken(act_, ("gainT",))
            split_hi(0)
            for t in range(MT):
                for half in range(2):
                    take(("memT", t, half), memT_hi[:, 4 * half:4 * half + 4, t * P:(t + 1) * P], frees=False)
                    if (t, half) == (1, 0):
                        split_hi(1)

            def row_squares(c):
                act_.wait_ge((mem_in + x_in)[c], 16)
                square(mem_t[:, c, :] if c < MT else x_t[:, c - MT, :], junk, ss[:, c:c + 1])

            def x_hi(t):
                for half in range(2):
                    take(("xT", t, half), h_hi[:, 4 * half:4 * half + 4, t * P:(t + 1) * P], frees=False)

            for n in range(N_MEMK, N_Q):
                split_hi(n + 2)
                for c in ROW_SUMS[n] if n < 6 else ():
                    row_squares(c)
                if n >= N_MEMV:
                    x_hi(n - N_MEMV)
                if n == 6:
                    for t in range(MT):
                        act_.wait_ge(pow_ready, ROOT_NTH[t])
                        take(("mk", t), mk_raw[:, t, :], ss[:, t:t + 1])
                if n == 7:
                    for t in range(MT):
                        take(("mv", t), m_v[:, t, :], ss[:, t:t + 1])

            def raws(name, dst, width):
                for t in range(TT):
                    take((name, t), dst[:, t, 0:width], columns=slice(0, width))

            def heads(ap, a):
                return ap.rearrange("p (a c) -> p a c", a=a)

            def keys(t):
                act_.wait_ge(pe_done, DONE[("kmT", t)])
                nc.scalar.activation(kT[:, :, t * P:(t + 1) * P], heads(bank[BANK[("kmT", t)]][:, 0:256], NKV),
                                     ACT.Copy, scale=kg)
                take(("kmT", t), mqT[:, 0:2, t * P:(t + 1) * P], mqg, columns=slice(256, 512))

            def exps(t):
                lo = 0 if t else CHUNK
                act_.wait_ge(maxed, t + 1)
                for hh in range(NH):
                    p = probs[:, hh, CHUNK + lo:256]
                    nc.scalar.activation(p, p, ACT.Exp, bias=top[:, hh:hh + 1], accum_out=den[:, hh:hh + 1])
                nc.scalar.activation(sink_e, sink_e, ACT.Exp).then_inc(expd, 1)

            def mem_exps(t):
                act_.wait_ge(mmaxed, t + 1)
                if t:
                    act_.wait_ge(pe_done, DONE[("mprobT", t - 1, 1)])
                for hh in range(MH):
                    ins = nc.scalar.activation(mprobs[:, hh, :], bank[BANK[("mscore", t, hh // 2)]]
                                               [:, hh % 2 * MEM:(hh % 2 + 1) * MEM], ACT.Exp,
                                               bias=mtop[:, hh:hh + 1], accum_out=mden[:, hh:hh + 1])
                    if hh % 2:
                        ins.then_inc(taken[BANK[("mscore", t, hh // 2)]], 1)

            def take_probs(t):
                for kt in ((0, 1) if t else (1,)):
                    take(("probT", t, kt, 0), probT[:, kt, 0, :, :].rearrange("p r c -> p (r c)"))

            def attend(t):
                take(("attn", t), a_hi[:, 4:8, t * P:(t + 1) * P], frees=False)

            def mem_attend(t):
                take(("mattn", t), a_hi[:, 8:12, t * P:(t + 1) * P], frees=False)

            for n in range(N_Q, N_CONV):
                split_hi(n + 2)
                if n == 10:
                    act_.wait_ge(params_done, 1)
                    for t in range(MT):
                        take(("mkT", t), mkT[:, :, t * P:(t + 1) * P], mkg)
                if n in (13, 14):
                    for t in (2 * (n - 13), 2 * (n - 13) + 1):
                        take(("qT", t), qT[:, :, t * P:(t + 1) * P], qg)
                if n == N_KVM - 1:
                    raws("q", raw_a, 512)
                if n == N_MQ2 - 1:
                    raws("kvm", raw_b, 512)
                if n == 16:
                    keys(0)
                    keys(1)
                if n == N_CONV - 1:
                    raws("mq2", raw_a, 256)
                    keys(2)
                    keys(3)
            for n in range(N_CONV, N_J):
                split_hi(n + 2)
                r, pair = (n - N_CONV) % 6, (n - N_CONV) // 6
                if n == 18:
                    exps(0)
                if n - 1 in MEM_SCORES:
                    mem_exps(MEM_SCORES.index(n - 1))
                if n - 1 in ATTEND:
                    exps(ATTEND.index(n - 1) + 1)
                if r < 2:
                    if pair:
                        act_.wait_ge(conv_x, r + 1)
                    take(("conv", n), temp[:, r, :])
                if n == 18:
                    for a in range(2):
                        take(("mq2T", a), mqT[:, 2:4, 2 * a * P:2 * (a + 1) * P].rearrange("p h (t c) -> p t h c", t=2),
                             mqg)
                if r >= 4:
                    c = 2 * pair + r - 4
                    wait_taken(act_, ("conv", n))
                    nc.scalar.activation(a_hi[:, c, :], temp[:, 2 + c % 2, :], ACT.Copy).then_inc(conv_hi, 1)
                if n in PROBS_AT:
                    take_probs(PROBS_AT.index(n))
                if n in MEM_PROBS_AT:
                    take(("mprobT", MEM_PROBS_AT.index(n), 0), mprobT[:, 0, :])
                if n in ATTEND:
                    attend(ATTEND.index(n))
                if n in MEM_ATTEND:
                    mem_attend(MEM_ATTEND.index(n))

            def merge_pair(i, last):
                for r in range(J_WT):
                    split_hi(N_J + r + 2, i, J_WT) if not last else split_hi(N_J + (J_IT - 1) * J_WT + r + 2)
                    if r < 6:
                        act_.wait_ge(pe_done, i * J_DONE + DONE0 + r + 1)
                        nc.scalar.activation(sig[:, r, :], bank[r % 4][:, :], ACT.Sigmoid,
                                             bias=bg_col[:, ds(i * 2 + (r // 2 * KD + r % 2), 1)])\
                            .then_inc(taken[r % 4], 1)
                    if last and r in (6, 7):
                        for j in range(3 * (r - 6), 3 * (r - 5)):
                            merged_split(j)

            def merged_split(j):
                if j == 0:
                    act_.wait_ge(pe_done, DONE0 + J_DONE * (J_IT - 1) + 6)
                if j % 2 == 0:
                    act_.wait_ge(merged_ready, j + 2)
                nc.scalar.activation(h_hi[:, j, :], merged[:, j * SEQ:(j + 1) * SEQ], ACT.Copy).then_inc(merged_hi, 1)

            with act_.Fori(0, J_IT - 1) as i:
                merge_pair(i, False)
                act_.wait_ge(taken[7], i + TAKEN0[7] + 1)
            merge_pair(J_IT - 1, True)
            merged_split(6)
            merged_split(7)

            def x2_squares(t, half, total):
                b = t + 4 * half
                act_.wait_ge(taken[b], TAKEN_WO[b] + 1)
                square(x2[:, t, half * 512:(half + 1) * 512], arena[:, 8192:8704], total[:, t:t + 1])

            def h2_hi(t):
                for half in range(2):
                    act_.wait_ge(pe_done, WO_AT[("h2T", t)] - 1 + half)
                    nc.scalar.activation(a_hi[:, 4 * half:4 * half + 4, t * P:(t + 1) * P],
                                         bank[2 * (t % 2) + half][:, :].rearrange("p (a c) -> p a c", a=4), ACT.Copy)\
                        .then_inc(hi_taken, 1)

            for n in range(N_WO + 2, N_WO + 8):
                split_hi(n)
            for t in range(TT):
                x2_squares(t, 0, ss2a)
            for t in range(TT):
                if t == TT - 1:
                    split_hi(N_UP)
                    split_hi(N_UP + 1)
                x2_squares(t, 1, ss2b)
                if t:
                    h2_hi(t - 1)
            h2_hi(TT - 1)

            def ring(m, i=0, wait=None):
                if wait is not None:
                    act_.wait_ge(pe_done, wait)
                nc.scalar.activation(aring_hi[:, m % 2 * 1024:(m % 2 + 1) * 1024],
                                     act[:, ds(i * 2048 + m * 1024, 1024)], ACT.Copy).then_inc(ring_hi, 1)

            def up_pair(i, last):
                for r in range(4):
                    if last:
                        split_hi(N_UP + 4 * (UP_IT - 1) + r + 2)
                    else:
                        split_hi(N_UP + r + 2, i, 4)
                    if r % 2:
                        act_.wait_ge(taken[3 + r], i + TAKEN_UP[3 + r] + 1)
                        nc.scalar.activation(temp[:, r - 1, :], temp[:, r - 1, :], ACT.Silu).then_inc(silu_ready, 1)
                    col = i * 2 + (r % 2 * FB + r // 2)
                    act_.wait_ge(pe_done, i * UP_DONE + DONE_UP + r + 1)
                    nc.scalar.activation(temp[:, r, :], bank[4 + r][:, :], ACT.Identity,
                                         bias=fb_col[:, ds(col, 1)], scale=fw_col[:, ds(col + 4 * FB, 1)])\
                        .then_inc(tap_ready, 1)

            with act_.Fori(0, UP_IT - 1) as i:
                up_pair(i, False)
                act_.wait_ge(act_ready, i * 2 + 2)
            act_.wait_ge(act_ready, 2)
            ring(0)
            up_pair(UP_IT - 1, True)

            ring(1)
            split_hi(N_DN + 2)
            split_hi(N_DN + 3)

            def down_pair(m, i):
                ring(m + 1, i, i * 4 + DONE_DN + 2 * m)
                split_hi(N_DN + 2 * m + 2, i, 4)
                split_hi(N_DN + 2 * m + 3, i, 4)

            with act_.Fori(0, DN_IT) as i:
                down_pair(1, i)
                down_pair(2, i)
            act_.wait_ge(act_ready, FB)
            m = FB // 2 - 2
            ring(m + 1, 0, DONE_DN + 2 * m)
            split_hi(N_END - 2)
            split_hi(N_END - 1)

        @block.vector
        def _(dve):
            chain = [0]

            def then(ins, base=0):
                chain[0] += 1
                ins.then_inc(dve_chain, 1)
                dve.wait_ge(dve_chain, base + chain[0])

            def split_lo(n, i=0, period=0):
                s = slot_of(n)
                dve.wait_ge(hi_ready, i * period + n + 1)
                if n < N_Q:
                    for k in range(2):
                        at = slice(k * 512, (k + 1) * 512)
                        ins = nc.vector.scalar_tensor_tensor(
                            out=w_lo[:, s, at], in0=stage[:, s, at], scalar=mem_gain_of(n, k),
                            in1=w_hi[:, s, at].bitcast(f32), op0=ALU.mult, op1=ALU.subtract)
                    ins.then_inc(lo_ready, 1)
                    return
                nc.vector.tensor_tensor(w_lo[:, s, :], stage[:, s, :], w_hi[:, s, :].bitcast(f32),
                                        ALU.subtract).then_inc(lo_ready, 1)

            hi_parts = [0]

            def take_lo(name, hi, lo):
                hi_parts[0] += 1
                dve.wait_ge(hi_taken, hi_parts[0])
                nc.vector.tensor_tensor(lo, bank[BANK[name]][:, :].rearrange("p (a c) -> p a c", a=4),
                                        hi.bitcast(f32), ALU.subtract).then_inc(taken[BANK[name]], 1)

            def variance(v, parts):
                for k, (c0, c1, width) in enumerate(parts):
                    ins = nc.vector.tensor_scalar(v[:, c0:c1], v[:, c0:c1], 1.0 / width, EPS, ALU.mult, ALU.add)
                    if k == len(parts) - 1:
                        ins.then_inc(var_ready, 1)

            powed = [MT + TT]

            def wait_pow():
                powed[0] += 1
                dve.wait_ge(pow_ready, powed[0])

            def x_norm(t):
                dve.wait_ge(pow_ready, ROOT_NTH[MT + t])
                nc.vector.scalar_tensor_tensor(out=x_t[:, t, :], in0=x_t[:, t, :], scalar=ss[:, MT + t:MT + t + 1],
                                               in1=gain_mix, op0=ALU.mult, op1=ALU.mult).then_inc(normed, 1)

            def head_norm(dst, src, v, shape, signal=True):
                a, w = shape
                ins = nc.vector.tensor_tensor(dst, src, v.unsqueeze(2).broadcast_to([P, a, w]), ALU.mult)
                if signal:
                    ins.then_inc(normed, 1)
                return ins

            def heads(ap, a):
                return ap.rearrange("p (a c) -> p a c", a=a)

            dve.wait_ge(pe_done, DONE[("gainT",)])
            nc.vector.tensor_copy(mem_gain, bank[BANK[("gainT",)]][:, 0:KD]).then_inc(taken[BANK[("gainT",)]], 1)
            wait_taken(dve, ("gainT",))
            split_lo(0)
            for t in range(MT):
                for half in range(2):
                    at = (slice(None), slice(4 * half, 4 * half + 4), slice(t * P, (t + 1) * P))
                    take_lo(("memT", t, half), memT_hi[at], memT_lo[at])
                    if (t, half) == (1, 0):
                        split_lo(1)

            for n in range(N_MEMK, N_Q):
                split_lo(n + 2)
                if n == 4:
                    dve.wait_ge(pe_done, DONE[("params",)])
                    nc.vector.tensor_copy(cols[:, 0:216], bank[BANK[("params",)]][:, 0:216])\
                        .then_inc(taken[BANK[("params",)]], 1)
                    wait_taken(dve, ("params",))
                    nc.vector.tensor_scalar(qg, qg, HD ** -0.5, None, ALU.mult)
                    nc.vector.tensor_scalar(mqg, mqg, MHD ** -0.5, None, ALU.mult).then_inc(params_done, 1)
                    dve.wait_ge(pe_done, DONE[("relvec",)])
                    nc.vector.tensor_copy(rel_row, bank[BANK[("relvec",)]][0:NH, 0:REL])\
                        .then_inc(taken[BANK[("relvec",)]], 1)
                if 1 <= n <= TT:
                    if n == 1:
                        dve.wait_ge(gain_mix_in, 16)
                    x_norm(n - 1)
                for c in ROW_SUMS[n] if n < 6 else ():
                    dve.wait_ge(squares, ROOT_NTH[c])
                    variance(ss, [(c, c + 1, D)])
                if n >= N_MEMV:
                    t = n - N_MEMV
                    for half in range(2):
                        at = (slice(None), slice(4 * half, 4 * half + 4), slice(t * P, (t + 1) * P))
                        take_lo(("xT", t, half), h_hi[at], h_lo[at])

            for n in range(N_Q, N_CONV):
                split_lo(n + 2)
                if n == 8:
                    for t in range(MT):
                        dve.wait_ge(sq_ready, t + 1)
                        then(nc.vector.tensor_reduce(out=mk_[:, t, :], in_=heads(temp[:, t, :], MH), op=ALU.add,
                                                     axis=AX.X))
                        variance(mk_[:, t, :], [(0, MH, MHD)])
                if n == 9:
                    for t in range(MT):
                        wait_pow()
                        head_norm(heads(mk_raw[:, t, :], MH), heads(mk_raw[:, t, :], MH), mk_[:, t, :], (MH, MHD))
                if n == 10:
                    dve.wait_ge(relflip_in, 16)
                    then(nc.vector.tensor_copy(bias, rel_flip[:, :, ::-1]))
                    nc.vector.memset(bias[0:CHUNK, :, 2 * CHUNK:WIN], MASKED)
                    then(nc.vector.memset(bias[CHUNK:P, :, 0:CHUNK], MASKED))
                if n == N_KVM - 1:
                    for t in range(TT):
                        dve.wait_ge(sq_ready, MT + t + 1)
                        then(nc.vector.tensor_reduce(out=hv[:, t, :], in_=heads(temp[:, t, :], NH), op=ALU.add,
                                                     axis=AX.X))
                        variance(hv[:, t, :], [(0, NH, HD)])
                    for t in range(TT):
                        wait_pow()
                        head_norm(heads(raw_a[:, t, :], NH), heads(raw_a[:, t, :], NH), hv[:, t, :], (NH, HD))
                if n == N_MQ2 - 1:
                    for t0 in (0, 2):
                        for t in (t0, t0 + 1):
                            dve.wait_ge(sq_ready, MT + TT + t + 1)
                            nc.vector.tensor_reduce(out=kv_[:, t, 0:2], in_=heads(temp[:, t, 0:P], 2),
                                                    op=ALU.add, axis=AX.X)
                            then(nc.vector.tensor_reduce(out=kv_[:, t, 2:4], in_=heads(temp[:, t, 256:512], 2),
                                                         op=ALU.add, axis=AX.X))
                            variance(kv_[:, t, :], [(0, 2, HD), (2, 4, MHD)])
                        for t in (t0, t0 + 1):
                            wait_pow()
                            for g in range(NKV):
                                nc.vector.tensor_tensor(
                                    temp[:, t, g * P:(g + 1) * P].rearrange("p (a c) -> p a c", a=2),
                                    raw_b[:, t, g * HD:(g + 1) * HD].unsqueeze(1).broadcast_to([P, 2, HD]),
                                    kv_[:, t, g:g + 1].unsqueeze(2).broadcast_to([P, 2, HD]), ALU.mult)
                            head_norm(heads(raw_b[:, t, 256:512], 2), heads(raw_b[:, t, 256:512], 2), kv_[:, t, 2:4],
                                      (2, MHD))
                if n == N_CONV - 1:
                    for t in range(TT):
                        dve.wait_ge(sq_ready, MT + 2 * TT + t + 1)
                        then(nc.vector.tensor_reduce(out=mq_[:, t, 0:2], in_=heads(temp[:, t, 256:512], 2), op=ALU.add,
                                                     axis=AX.X))
                        variance(mq_[:, t, 0:2], [(0, 2, MHD)])
                    for t in range(TT):
                        wait_pow()
                        head_norm(heads(raw_a[:, t, 0:256], 2), heads(raw_a[:, t, 0:256], 2), mq_[:, t, 0:2], (2, MHD))

            def tops(t):
                lo = 0 if t else CHUNK
                dve.wait_ge(zeroed, 2)
                if t:
                    dve.wait_ge(pe_done, DONE[("probT", t - 1, 1, 1)])
                else:
                    dve.wait_ge(sink_in, 16)
                for g in range(NKV):
                    for r in range(2):
                        name = ("score", t, g, r)
                        dve.wait_ge(pe_done, DONE[name])
                        nc.vector.tensor_tensor(probs[:, 4 * g + r:4 * g + r + 3:2, CHUNK + lo:256],
                                                heads(bank[BANK[name]][:, 0:2 * WIN], 2)[:, :, lo:WIN],
                                                bias[:, 4 * g + r:4 * g + r + 3:2, lo:WIN], ALU.add)\
                            .then_inc(taken[BANK[name]], 1)
                for g in range(NKV):
                    for r in range(2):
                        name = ("score", t, g, r)
                        dve.wait_ge(taken[BANK[name]], NTH[name])
                then(nc.vector.tensor_reduce(out=top, in_=probs[:, :, CHUNK + lo:256], op=ALU.max, axis=AX.X))
                then(nc.vector.tensor_tensor(top, top, sink, ALU.max))
                then(nc.vector.tensor_scalar(top, top, -1.0, None, ALU.mult))
                nc.vector.tensor_tensor(sink_e, sink, top, ALU.add).then_inc(maxed, 1)

            def sums(t):
                dve.wait_ge(expd, t + 1)
                then(nc.vector.tensor_tensor(den, den, sink_e, ALU.add))
                nc.vector.reciprocal(den, den).then_inc(recip, 1)

            def mem_tops(t):
                for a in range(2):
                    dve.wait_ge(pe_done, DONE[("mscore", t, a)])
                    pair = heads(bank[BANK[("mscore", t, a)]][:, :], 2)
                    ins = nc.vector.tensor_reduce(out=mtop[:, 2 * a:2 * a + 2], in_=pair, op=ALU.max, axis=AX.X)
                then(ins)
                nc.vector.tensor_scalar(mtop, mtop, -1.0, None, ALU.mult).then_inc(mmaxed, 1)

            def mem_sums(t):
                for a in range(2):
                    wait_taken(dve, ("mscore", t, a))
                nc.vector.reciprocal(mden, mden).then_inc(mrecip, 1)

            def take_probs(t):
                for kt in ((0, 1) if t else (1,)):
                    name = ("probT", t, kt, 1)
                    dve.wait_ge(pe_done, DONE[name])
                    nc.vector.tensor_copy(probT[:, kt, 1, :, :].rearrange("p r c -> p (r c)"), bank[BANK[name]][:, :])\
                        .then_inc(taken[BANK[name]], 1)

            def take_mem_probs(t):
                name = ("mprobT", t, 1)
                dve.wait_ge(pe_done, DONE[name])
                nc.vector.tensor_copy(mprobT[:, 1, :], bank[BANK[name]][:, :]).then_inc(taken[BANK[name]], 1)

            def attend(t):
                at = (slice(None), slice(4, 8), slice(t * P, (t + 1) * P))
                take_lo(("attn", t), a_hi[at], a_lo[at])

            def mem_attend(t):
                at = (slice(None), slice(8, 12), slice(t * P, (t + 1) * P))
                take_lo(("mattn", t), a_hi[at], a_lo[at])

            tops(0)
            for n in range(N_CONV, N_J):
                split_lo(n + 2)
                r, pair = (n - N_CONV) % 6, (n - N_CONV) // 6
                name = ("conv", n)
                if n - 1 in MEM_SCORES:
                    mem_tops(MEM_SCORES.index(n - 1))
                if r in (2, 3):
                    c, k = 2 * pair + r - 2, r - 2
                    wait_taken(dve, ("conv", n - 2))
                    dve.wait_ge(pe_done, DONE[name])
                    nc.vector.tensor_tensor(temp[:, k, :], bank[BANK[name]][:, :], temp[:, k, :], ALU.mult)\
                        .then_inc(taken[BANK[name]], 1)
                    dve.wait_ge(taken[BANK[name]], NTH[name])
                    w = [cw_col[:, a * CB + c:a * CB + c + 1] for a in range(3)]
                    then(nc.vector.tensor_scalar(temp[:, 2 + k, :], temp[:, k, :], w[2], None, ALU.mult))
                    then(nc.vector.scalar_tensor_tensor(out=temp[:, 2 + k, 1:SEQ], in0=temp[:, k, 0:SEQ - 1],
                                                        scalar=w[1], in1=temp[:, 2 + k, 1:SEQ], op0=ALU.mult, op1=ALU.add))
                    nc.vector.scalar_tensor_tensor(out=temp[:, 2 + k, 2:SEQ], in0=temp[:, k, 0:SEQ - 2], scalar=w[0],
                                                   in1=temp[:, 2 + k, 2:SEQ], op0=ALU.mult, op1=ALU.add)\
                        .then_inc(conv_x, 1)
                if r >= 4:
                    c, k = 2 * pair + r - 4, r - 4
                    dve.wait_ge(pe_done, DONE[name])
                    dve.wait_ge(conv_x, c + 1)
                    nc.vector.tensor_tensor(temp[:, 2 + k, :], bank[BANK[name]][:, :], temp[:, 2 + k, :], ALU.mult)\
                        .then_inc(taken[BANK[name]], 1)
                    dve.wait_ge(conv_hi, c + 1)
                    nc.vector.tensor_tensor(a_lo[:, c, :], temp[:, 2 + k, :], a_hi[:, c, :].bitcast(f32),
                                            ALU.subtract).then_inc(conv_lo, 1)
                if n == 18:
                    sums(0)
                if n - 1 in ATTEND:
                    sums(ATTEND.index(n - 1) + 1)
                if n - 1 in MEM_SCORES:
                    mem_sums(MEM_SCORES.index(n - 1))
                if n in PROBS_AT:
                    take_probs(PROBS_AT.index(n))
                if n in MEM_PROBS_AT:
                    take_mem_probs(MEM_PROBS_AT.index(n))
                if n in ATTEND:
                    attend(ATTEND.index(n))
                    if n != ATTEND[-1]:
                        tops(ATTEND.index(n) + 1)
                if n in MEM_ATTEND:
                    mem_attend(MEM_ATTEND.index(n))

            def merge_pair(i, base, last):
                for r in range(J_WT):
                    if last:
                        split_lo(N_J + (J_IT - 1) * J_WT + r + 2)
                    else:
                        split_lo(N_J + r + 2, i, J_WT)
                    for jj in range(2) if r >= 6 else ():
                        b = 2 + 2 * (r - 6) + jj
                        gate_b = (2 * (r - 6) + jj) % 4
                        dve.wait_ge(taken[gate_b], i * J_TAKEN[gate_b] + TAKEN0[gate_b] + (2 if r == 8 else 1))
                        dve.wait_ge(pe_done, i * J_DONE + DONE0 + 6 + 2 * (r - 6) + jj + 1)
                        m = merged[:, ds(i * 1024 + jj * SEQ, SEQ)]
                        g = sig[:, 2 * (r - 6) + jj, :]
                        if r == 6:
                            nc.vector.tensor_tensor(m, bank[b][:, :], g, ALU.mult).then_inc(taken[b], 1)
                            continue
                        nc.vector.tensor_tensor(merge_tmp[:, jj, :], bank[b][:, :], g, ALU.mult).then_inc(taken[b], 1)
                        dve.wait_ge(taken[b], i * J_TAKEN[b] + TAKEN0[b] + 1)
                        if r == 7:
                            dve.wait_ge(taken[2 + jj], i * J_TAKEN[2] + TAKEN0[2 + jj] + 2)
                            then(nc.vector.tensor_tensor(m, m, merge_tmp[:, jj, :], ALU.add), base)
                        else:
                            nc.vector.tensor_tensor(m, m, merge_tmp[:, jj, :], ALU.add).then_inc(merged_ready, 1)
                    if last and r in (7, 8):
                        for j in range(3 * (r - 7), 3 * (r - 6)):
                            merged_split(j)

            def merged_split(j):
                dve.wait_ge(merged_hi, j + 1)
                nc.vector.tensor_tensor(h_lo[:, j, :], merged[:, j * SEQ:(j + 1) * SEQ], h_hi[:, j, :].bitcast(f32),
                                        ALU.subtract).then_inc(merged_lo, 1)

            with dve.Fori(0, J_IT - 1) as i:
                merge_pair(i, i * 2, False)
            chain[0] += 2 * (J_IT - 2)
            merge_pair(J_IT - 1, 0, True)
            merged_split(6)
            merged_split(7)

            for n in range(N_WO + 2, N_WO + 8):
                split_lo(n)
            dve.wait_ge(x_again, 16)
            dve.wait_ge(ffn_gain_in, 16)

            def add_x2(t, half):
                b = t + 4 * half
                dve.wait_ge(pe_done, WO_AT[("wo", t)] if half else DONE_WO + 4 + t)
                x2_half = x2[:, t, half * 512:(half + 1) * 512]
                nc.vector.tensor_tensor(x2_half, bank[b][:, :], x2_half, ALU.add).then_inc(taken[b], 1)

            def h2_norm(t):
                dve.wait_ge(squares, MT + TT + TT + t + 1)
                then(nc.vector.tensor_tensor(ss2a[:, t:t + 1], ss2a[:, t:t + 1], ss2b[:, t:t + 1], ALU.add))
                variance(ss2a[:, t:t + 1], [(0, 1, D)])
                wait_pow()
                if t >= 2:
                    dve.wait_ge(pe_done, WO_AT[("h2T", t - 2)])
                nc.vector.scalar_tensor_tensor(out=temp2[:, t % 2, :], in0=x2[:, t, :], scalar=ss2a[:, t:t + 1],
                                               in1=gain_ffn, op0=ALU.mult, op1=ALU.mult).then_inc(normed, 1)

            def h2_lo(t):
                for half in range(2):
                    hi_parts[0] += 1
                    dve.wait_ge(hi_taken, hi_parts[0])
                    b = 2 * (t % 2) + half
                    at = (slice(None), slice(4 * half, 4 * half + 4), slice(t * P, (t + 1) * P))
                    nc.vector.tensor_tensor(a_lo[at], bank[b][:, :].rearrange("p (a c) -> p a c", a=4),
                                            a_hi[at].bitcast(f32), ALU.subtract).then_inc(taken[b], 1)

            for t in range(TT):
                add_x2(t, 0)
            for t in range(TT):
                if t == TT - 1:
                    split_lo(N_UP)
                    split_lo(N_UP + 1)
                add_x2(t, 1)
                h2_norm(t)
                if t:
                    h2_lo(t - 1)
            h2_lo(TT - 1)

            def ring(m, i=0):
                dve.wait_ge(ring_hi, i * 2 + m + 1)
                part = slice(m % 2 * 1024, (m % 2 + 1) * 1024)
                nc.vector.tensor_tensor(aring_lo[:, part], act[:, ds(i * 2048 + m * 1024, 1024)],
                                        aring_hi[:, part].bitcast(f32), ALU.subtract).then_inc(ring_lo, 1)

            def up_pair(i, base, last):
                for r in range(4):
                    if last:
                        split_lo(N_UP + 4 * (UP_IT - 1) + r + 2)
                    else:
                        split_lo(N_UP + r + 2, i, 4)
                    b, u = 4 + r, temp[:, r, :]
                    col = i * 2 + (r % 2 * FB + r // 2)
                    dve.wait_ge(tap_ready, i * 4 + r + 1)
                    then(nc.vector.scalar_tensor_tensor(out=u[:, 1:SEQ], in0=bank[b][:, 0:SEQ - 1],
                                                        scalar=fw_col[:, ds(col + 2 * FB, 1)], in1=u[:, 1:SEQ],
                                                        op0=ALU.mult, op1=ALU.add), base)
                    nc.vector.scalar_tensor_tensor(out=u[:, 2:SEQ], in0=bank[b][:, 0:SEQ - 2],
                                                   scalar=fw_col[:, ds(col, 1)], in1=u[:, 2:SEQ],
                                                   op0=ALU.mult, op1=ALU.add).then_inc(taken[b], 1)
                    if r % 2:
                        dve.wait_ge(taken[b], i + TAKEN_UP[b] + 1)
                        dve.wait_ge(silu_ready, i * 2 + r // 2 + 1)
                        nc.vector.tensor_tensor(act[:, ds(i * 1024 + r // 2 * SEQ, SEQ)], temp[:, r - 1, :], u,
                                                ALU.mult).then_inc(act_ready, 1)

            with dve.Fori(0, UP_IT - 1) as i:
                up_pair(i, i * 4, False)
            chain[0] += 4 * (UP_IT - 2)
            ring(0)
            up_pair(UP_IT - 1, 0, True)

            ring(1)
            split_lo(N_DN + 2)
            split_lo(N_DN + 3)

            def down_pair(m, i):
                ring(m + 1, i)
                split_lo(N_DN + 2 * m + 2, i, 4)
                split_lo(N_DN + 2 * m + 3, i, 4)

            with dve.Fori(0, DN_IT) as i:
                down_pair(1, i)
                down_pair(2, i)
            ring(FB // 2 - 1)
            split_lo(N_END - 2)
            split_lo(N_END - 1)

            for t in range(TT):
                for half in range(2):
                    dve.wait_ge(pe_done, DONE_DN + FB - 2 + 2 * t + half + 1)
                    x2_half = x2[:, t, half * 512:(half + 1) * 512]
                    nc.vector.tensor_tensor(x2_half, bank[t + 4 * half][:, :], x2_half, ALU.add).then_inc(final, 1)


INPUTS = ["x", "mem", "rel_bias", "norm_mix", "norm_mem", "norm_ffn", "w_in", "b_gate", "conv_w", "q_norm", "k_norm",
          "sinks", "mq_norm", "mk_norm", "w_mem_kv", "w_br_conv", "w_br_attn", "w_br_mem", "w_o", "w_up",
          "ffn_conv_w", "ffn_conv_b", "w_down"]


def shape_constants():
    import numpy as np

    rel = (WIN - 1 - CHUNK) - np.arange(REL)
    buckets, max_distance = 32, 128
    nb = buckets // 2
    n, exact = np.abs(rel), nb // 2
    large = exact + (np.log(np.maximum(n, 1) / exact) / np.log(max_distance / exact) * (nb - exact)).astype(np.int32)
    bucket = (rel > 0) * nb + np.where(n < exact, n, np.minimum(large, nb - 1))
    one = (np.arange(buckets)[:, None] == bucket[None, :]).astype(np.float32)
    return {"eye": np.eye(P, dtype=np.float32), "bucket_of": one}


def kernel(**inputs):
    import numpy as _np
    import concourse.bacc as _bacc
    from concourse import mybir as _mybir
    from concourse.bass_utils import run_bass_kernel_spmd as _run

    nc = _bacc.Bacc("TRN2", target_bir_lowering=False, num_devices=1)
    arrays, args = {}, []
    for name, a in [(n, inputs[n]) for n in INPUTS] + list(shape_constants().items()):
        a = _np.ascontiguousarray(a)
        arrays[f"in_{name}_dram"] = a
        args.append(nc.dram_tensor(f"in_{name}_dram", a.shape, _mybir.dt.from_np(a.dtype), kind="ExternalInput").ap())
    args.append(nc.dram_tensor("out_dram", (1, SEQ, D), _mybir.dt.float32, kind="ExternalOutput").ap())
    trunk(nc, *args)
    r = _run(nc, [arrays], core_ids=[0])
    return r.results[0]["out_dram"]
```
